# Optimizing a Trainium2 kernel written in Bass

```python
import jax, jax.numpy as jnp
from jax import lax
import numpy as np

D_MODEL = 2048
BATCH = 1
SEQ = 512
DEPTH = 2

CHUNK = 64
Q_BLOCK = 128
PLE_DIM = 256
HEAD_DIM = 128
N_HEADS_FOX = D_MODEL // HEAD_DIM
EXPAND = 128
N_HEADS_HG = D_MODEL // EXPAND
HG_V_DIM = D_MODEL // N_HEADS_HG
EPS = 1e-6
NEG = -1e30

kernel_name = "fox_hgrn2_interleaved_sandwich_ple"

def rms_norm(x, g):
    xf = x.astype(jnp.float32)
    y = xf * lax.rsqrt(jnp.mean(xf * xf, axis=-1, keepdims=True) + EPS)
    return (y * g.astype(jnp.float32)).astype(x.dtype)

def fox_mixer(xn, w_in, b_f, g_q, g_k, w_out):
    B, S, D = xn.shape
    H, Dh = N_HEADS_FOX, HEAD_DIM
    proj = xn @ w_in
    q, k, v, z, f_logit = jnp.split(proj, [D, 2 * D, 3 * D, 4 * D], axis=-1)
    q = rms_norm(q.reshape(B, S, H, Dh), g_q).transpose(0, 2, 1, 3)
    k = rms_norm(k.reshape(B, S, H, Dh), g_k).transpose(0, 2, 1, 3)
    v = v.reshape(B, S, H, Dh).transpose(0, 2, 1, 3)
    log_f = jax.nn.log_sigmoid((f_logit + b_f).astype(jnp.float32))
    c = jnp.cumsum(log_f, axis=1).transpose(0, 2, 1)
    nb = S // Q_BLOCK
    q_blocks = q.reshape(B, H, nb, Q_BLOCK, Dh).transpose(2, 0, 1, 3, 4)
    c_blocks = c.reshape(B, H, nb, Q_BLOCK).transpose(2, 0, 1, 3)
    kpos = jnp.arange(S)
    scale = 1.0 / np.sqrt(Dh).astype(np.float32)

    def attend(args):
        qb, cqb, bid = args
        qpos = bid * Q_BLOCK + jnp.arange(Q_BLOCK)
        s = jnp.einsum('bhqd,bhkd->bhqk', qb, k).astype(jnp.float32) * scale
        s = s + (cqb[..., :, None] - c[:, :, None, :])
        mask = kpos[None, :] <= qpos[:, None]
        s = jnp.where(mask, s, NEG)
        prob = jax.nn.softmax(s, axis=-1)
        return jnp.einsum('bhqk,bhkd->bhqd', prob.astype(v.dtype), v).astype(v.dtype)

    o = lax.map(attend, (q_blocks, c_blocks, jnp.arange(nb)))
    o = o.transpose(1, 0, 3, 2, 4).reshape(B, S, D)
    return (o * jax.nn.silu(z)) @ w_out

def hgrn2_mixer(xn, w_in, lb, g_o, w_out):
    B, S, D = xn.shape
    H, dk, dv = N_HEADS_HG, EXPAND, HG_V_DIM
    nc = S // CHUNK
    proj = xn @ w_in
    q, f_logit, i_in, z = jnp.split(proj, 4, axis=-1)
    q = jax.nn.silu(q.astype(jnp.float32))
    forget = lb + (1.0 - lb) * jax.nn.sigmoid(f_logit.astype(jnp.float32))
    k = 1.0 - forget
    g = jnp.log(forget)

    def to_chunks(t, hd):
        return t.reshape(B, nc, CHUNK, H, hd).transpose(1, 0, 3, 2, 4)

    qc, kc, gc = to_chunks(q, dk), to_chunks(k, dk), to_chunks(g, dk)
    vc = to_chunks(i_in.astype(jnp.float32), dv)
    causal = jnp.tril(jnp.ones((CHUNK, CHUNK), dtype=bool))

    def step(state, inp):
        qq, kk, vv, gg = inp
        b = jnp.cumsum(gg, axis=2)
        inter = jnp.einsum('bhtd,bhdv->bhtv', qq * jnp.exp(b), state)
        diff = b[:, :, :, None, :] - b[:, :, None, :, :]
        decay = jnp.exp(jnp.where(causal[:, :, None], diff, -jnp.inf))
        att = jnp.einsum('bhtd,bhsd,bhtsd->bhts', qq, kk, decay)
        intra = jnp.einsum('bhts,bhsv->bhtv', att, vv)
        b_last = b[:, :, -1:, :]
        new_state = jnp.exp(b_last[:, :, 0, :])[..., None] * state + jnp.einsum(
            'bhsd,bhsv->bhdv', kk * jnp.exp(b_last - b), vv)
        return new_state, inter + intra

    s0 = jnp.zeros((B, H, dk, dv), jnp.float32)
    _, o = lax.scan(step, s0, (qc, kc, vc, gc))
    o = o.transpose(1, 0, 3, 2, 4).reshape(B, S, H, dv)
    o = rms_norm(o, g_o).reshape(B, S, D).astype(xn.dtype)
    return (o * jax.nn.silu(z)) @ w_out

def setup_inputs(seed: int = 0) -> dict:
    key = jax.random.key(seed)
    ks = jax.random.split(key, 16)
    D, H = D_MODEL, N_HEADS_FOX
    n_fox = (DEPTH + 1) // 2
    n_hg = DEPTH // 2
    nrm = lambda k, shape, fan: jax.random.normal(k, shape, jnp.float32) * fan ** -0.5
    gain = lambda k, shape: 1.0 + 0.05 * jax.random.normal(k, shape, jnp.float32)
    return {
        "x": jax.random.normal(ks[0], (BATCH, SEQ, D), jnp.float32),
        "p": jax.random.normal(ks[1], (DEPTH, BATCH, SEQ, PLE_DIM), jnp.float32),
        "w_in_fox": nrm(ks[2], (n_fox, D, 4 * D + H), D),
        "b_f_fox": jax.random.uniform(ks[3], (n_fox, H), jnp.float32, 1.0, 4.0),
        "g_q_fox": gain(ks[4], (n_fox, HEAD_DIM)),
        "g_k_fox": gain(ks[5], (n_fox, HEAD_DIM)),
        "w_out_fox": nrm(ks[6], (n_fox, D, D), D),
        "w_in_hg": nrm(ks[7], (n_hg, D, 4 * D), D),
        "lb_logits": 0.1 * jax.random.normal(ks[8], (DEPTH, D), jnp.float32),
        "g_o_hg": gain(ks[9], (n_hg, HG_V_DIM)),
        "w_out_hg": nrm(ks[10], (n_hg, D, D), D),
        "pre_norm": gain(ks[11], (DEPTH, D)),
        "post_norm": gain(ks[12], (DEPTH, D)),
        "w_pe": nrm(ks[13], (DEPTH, PLE_DIM, D), PLE_DIM),
        "w_pg": nrm(ks[14], (DEPTH, D, D), D),
    }

def reference(x, p, w_in_fox, b_f_fox, g_q_fox, g_k_fox, w_out_fox, w_in_hg,
              lb_logits, g_o_hg, w_out_hg, pre_norm, post_norm, w_pe, w_pg):
    gam = jax.nn.softmax(lb_logits.astype(jnp.float32), axis=0)
    lower_bounds = jnp.cumsum(gam, axis=0) - gam[0:1]
    h = x
    for i in range(DEPTH):
        xn = rms_norm(h, pre_norm[i])
        if i % 2 == 0:
            j = i // 2
            y = fox_mixer(xn, w_in_fox[j], b_f_fox[j], g_q_fox[j], g_k_fox[j], w_out_fox[j])
        else:
            j = i // 2
            y = hgrn2_mixer(xn, w_in_hg[j], lower_bounds[i], g_o_hg[j], w_out_hg[j])
        h = h + rms_norm(y, post_norm[i])
        pe = p[i].astype(h.dtype) @ w_pe[i]
        h = h + pe * jax.nn.sigmoid(h @ w_pg[i])
    return h


_drawn_inputs = setup_inputs


def setup_inputs(seed=0):
    import zlib

    import numpy as np

    out = dict(_drawn_inputs(seed))
    spreads = {}
    factors = {'lb_logits': 8.0}
    for name, (base, spread) in spreads.items():
        noise = np.random.default_rng([zlib.crc32(name.encode()), seed]).standard_normal(out[name].shape)
        drawn = base * np.exp(spread * noise) if base else spread * noise
        out[name] = __import__('jax').numpy.asarray(drawn.astype(out[name].dtype))
    for name, factor in factors.items():
        out[name] = (out[name] * factor).astype(out[name].dtype)
    return out
```

```python
from contextlib import ExitStack

import concourse.bass as bass
from concourse import mybir

F32 = mybir.dt.float32
F32R = mybir.dt.float32r
U8 = mybir.dt.uint8
ALU = mybir.AluOpType
ACT = mybir.ActivationFunctionType
AX = mybir.AxisListType

P = 128
S = 512
D = 2048
KT = D // P
TB = S // P
H = D // P
PLE = 256
PK = PLE // P
EPS = 1e-6
NEG = -1e30
LEVELS = 7

UB = 8
UPT = KT // UB
PE_UNITS = PK * KT // UB
RAW, RING = 2, 4
HI_AHEAD, LO_AHEAD = 3, 2
U_PE = 0
U_F = U_PE + 2 * PE_UNITS
U_FOX = U_F + UPT
U_OUT = [U_FOX + 4 * UPT * H, 0]
U_PG = [U_OUT[0] + UPT * KT, 0]
U_HG = U_PG[0] + UPT * KT
U_OUT[1] = U_HG + 4 * UPT * H
U_PG[1] = U_OUT[1] + UPT * KT
U_END = U_PG[1] + UPT * KT

T_PE = 0
T_F = T_PE + 2 * KT
T_FOX = T_F + 1
T_OUT = [T_FOX + 4 * H, 0]
T_PG = [T_OUT[0] + KT, 0]
T_HG = T_PG[0] + KT
T_OUT[1] = T_HG + 4 * H
T_PG[1] = T_OUT[1] + KT
N_HG = T_FOX + 4 * H

G_PRE, G_POST, G_LB, G_Q, G_K, G_O, G_ROWS = 0, 2 * KT, 4 * KT, 6 * KT, 6 * KT + 1, 6 * KT + 2, 6 * KT + 3


def trunk(nc, x, p, w_in_fox, b_f_fox, g_q_fox, g_k_fox, w_out_fox, w_in_hg, lb_logits, g_o_hg,
          w_out_hg, pre_norm, post_norm, w_pe, w_pg, c_ident, c_causal, c_levels, out):
    pe_scr = nc.dram_tensor("pe_scr", (2 * KT, P, S), F32, kind="Internal").ap()
    c_scr = nc.dram_tensor("c_scr", (H, S), F32, kind="Internal").ap()

    def rows_of(w):
        return w.rearrange("(k p) n -> p k n", p=P)

    wf, wh = rows_of(w_in_fox[0]), rows_of(w_in_hg[0])
    wo = [rows_of(w_out_fox[0]), rows_of(w_out_hg[0])]
    wg = [rows_of(w_pg[i]) for i in range(2)]
    x_tok = x[0].rearrange("(t p) n -> p t n", p=P)
    out_tok = out[0].rearrange("(t p) n -> p t n", p=P)

    ctx = ExitStack()
    with ctx:
        def sb(name, shape, dt=F32):
            return ctx.enter_context(nc.sbuf_tensor(name, shape, dt))

        def sem(name):
            return ctx.enter_context(nc.semaphore(name))

        ctx.enter_context(nc.allow_non_contiguous_dma(reason="one column of forget biases"))

        hT = sb("hT", [P, KT, S])
        xhi = sb("xhi", [P, KT, S], F32R)
        xlo = sb("xlo", [P, KT, S], F32R)
        yT = sb("yT", [P, KT, S])
        raw = sb("raw", [P, RAW, UB * P])
        whi = sb("whi", [P, RING, UB, P], F32R)
        wlo = sb("wlo", [P, RING, UB, P], F32R)
        rinv = sb("rinv", [P, S])
        ident = sb("ident", [P, P])
        ones = sb("ones", [P, P])
        causal = sb("causal", [P, P])
        levels = sb("levels", [P, LEVELS, S // 2], U8)
        gcol = sb("gcol", [P, P])
        lbc = sb("lbc", [P, 6, KT])
        cq = sb("cq", [P, TB, 32])
        small = sb("small", [P, 16])
        eps_c, one_c, bf_c = small[:, 0:1], small[:, 1:2], small[:, 2:3]
        negm, rsum = small[:, 4:8], small[:, 8:12]
        work = sb("work", [P, 15 * S])

        def wk(i, n=1):
            return work[:, i * S:(i + n) * S]

        q_t, k_t, v_t, z_t, tz_t, vtok = wk(0), wk(1), wk(2), wk(3), wk(4), wk(14)
        sqq, sqk, ckb, ckm = wk(5), wk(6), wk(7), wk(8)
        prob, probT = work[:, 9 * S:9 * S + 1280], work[:, 9 * S + 1280:9 * S + 2560]
        prob_at = [0, 128, 384, 768]
        probT_at = [0, 512, 896, 1152]
        osq, f_t, tree, att, kst, st, o_t, tq_t = (wk(i) for i in range(5, 13))
        sq2, acc = [wk(5), wk(6)], wk(13)
        tg2, pe2, hout2, ostage2 = [wk(0), wk(1)], [wk(2), wk(3)], [wk(7), wk(8)], [wk(9), wk(10)]
        xstage = [wk(i) for i in range(4)]
        pstage = [wk(7, 2), wk(9, 2)]
        pe_tile = [wk(12), wk(4)]
        grow = wk(11)[:, 0:P]
        level_in = work[:, 11 * S + P:11 * S + P + LEVELS * P // 2]
        fl, fa, fc, fone = wk(7), wk(8), wk(9), wk(10)
        FR = slice(P - 32, P)

        bank = [ctx.enter_context(nc.psum_tensor(f"bank{i}", [P, S], F32)) for i in range(8)]

        w_loaded = [sem(f"w_loaded{i}") for i in range(RAW)]
        hi_done, lo_done, w_used = sem("hi_done"), sem("lo_done"), sem("w_used")
        embed_done, tile_out = sem("embed_done"), sem("tile_out")
        xhi_done, x_ready = sem("xhi_done"), sem("x_ready")
        acc_zero, sq_done, acc_step = sem("acc_zero"), sem("sq_done"), sem("acc_step")
        norm_done, norm_rms, norm_ready = sem("norm_done"), sem("norm_rms"), sem("norm_ready")
        y_ready, yo_ready, yn_ready, hn_ready = sem("y_ready"), sem("yo_ready"), sem("yn_ready"), sem("hn_ready")
        tg_ready, h_new = sem("tg_ready"), sem("h_new")
        const_in, const_set, bias_in = sem("const_in"), sem("const_set"), sem("bias_in")
        p_in, pt_p, phi_done, p_ready = sem("p_in"), sem("p_turned"), sem("phi_done"), sem("p_ready")
        x_in = [sem(f"x_in{i}") for i in range(4)]
        x_turned, h_ready = sem("x_turned"), sem("h_ready")
        g_turned, g_ready = sem("g_turned"), sem("g_ready")
        lb_sem, lb_exp = sem("lb_step"), sem("lb_exp")
        pe_stored = [sem("pe_stored0"), sem("pe_stored1")]
        pe_in = [sem("pe_in0"), sem("pe_in1")]
        f_pre, f_exp, f_ln, f_cum, f_turned, cq_ready, c_stored = (
            sem(n) for n in ("f_pre", "f_exp", "f_ln", "f_cum", "f_turned", "cq_ready", "c_stored"))
        sq_ready, stats_done, rms_ready, qk_ready = sem("sq_ready"), sem("stats_done"), sem("rms_ready"), sem("qk_ready")
        vt_done, vtok_ready, tz_ready, zs_ready = sem("vt_done"), sem("vtok_ready"), sem("tz_ready"), sem("zs_ready")
        ck_in, ckm_ready = sem("ck_in"), sem("ckm_ready")
        scores_done, negm_ready, exp_ready = sem("scores_done"), sem("negm_ready"), sem("exp_ready")
        probs_ready, pt_done, pt_ready, pv_done = sem("probs_ready"), sem("pt_done"), sem("pt_ready"), sem("pv_done")
        hg_vt, hg_vtok, hg_tz = sem("hg_vt"), sem("hg_vtok"), sem("hg_tz")
        hg_qk, diag_done, level_ready, level_done, att_ready = (
            sem(n) for n in ("hg_qk", "diag_done", "level_ready", "level_done", "att_ready"))
        kst_done, kst_ready, u_done, state_ready = sem("kst_done"), sem("kst_ready"), sem("u_done"), sem("state_ready")
        ot_done, o_ready, osq_ready, ostat_done, orms_ready = (
            sem(n) for n in ("ot_done", "o_ready", "osq_ready", "ostat_done", "orms_ready"))
        thf_ready, tq_ready = sem("thf_ready"), sem("tq_ready")
        outT_done, out_staged = sem("outT_done"), sem("out_staged")
        out_stored = [sem("out_stored0"), sem("out_stored1")]
        v_step = sem("v_step")

        def wait(eng, s, value):
            if not (isinstance(value, int) and value <= 0):
                eng.wait_ge(s, value)

        def loop(eng, first, last, body):
            with eng.Fori(first, last) as i:
                body(i)

        block = ctx.enter_context(nc.Block())

        @block.sync
        def _(sp):
            def load(u, i, per, src, k=UB):
                n = u + per * i
                if not isinstance(n, int) or n >= RAW:
                    sp.wait_ge(lo_done, n - RAW + 1)
                dst = raw[:, u % RAW, :].rearrange("p (k n) -> p k n", k=k)
                sp.dma_start(dst, src).then_inc(w_loaded[u % RAW], 16)

            def tile_units(u, i, per, w, col):
                for j in range(UPT):
                    load(u + j, i, per, w[:, UB * j:UB * (j + 1), bass.ds(col, P)])

            for i in range(2):
                we = rows_of(w_pe[i])
                for j in range(PE_UNITS):
                    load(U_PE + j, i, PE_UNITS, we[:, :, 4 * P * j:4 * P * (j + 1)], k=PK)
            tile_units(U_F, 0, 0, wf, 4 * D + H - P)

            def fox_head(n):
                for j in range(4):
                    tile_units(U_FOX + UPT * j, n - 1, 4 * UPT, wf, n * P + (j * D - P))

            def hg_head(n):
                for j, part in enumerate((2, 1, 0, 3)):
                    tile_units(U_HG + UPT * j, n - 1, 4 * UPT, wh, n * P + (part * D - P))

            def square(u, w):
                def pair(i):
                    for j in range(2):
                        tile_units(u + UPT * j, i, 2 * UPT, w, (2 * i + j) * P)
                loop(sp, 1, KT // 2 + 1, lambda i: pair(i - 1))

            loop(sp, 1, H + 1, fox_head)
            square(U_OUT[0], wo[0])
            square(U_PG[0], wg[0])
            loop(sp, 1, H + 1, hg_head)
            square(U_OUT[1], wo[1])
            square(U_PG[1], wg[1])

        @block.gpsimd
        def _(pool):
            for dst, src in ((ident[:, :], c_ident), (causal[:, :], c_causal),
                             (level_in, c_levels),
                             (grow[G_PRE:G_PRE + 2 * KT, :], pre_norm.rearrange("l (k p) -> (l k) p", p=P)),
                             (grow[G_POST:G_POST + 2 * KT, :], post_norm.rearrange("l (k p) -> (l k) p", p=P)),
                             (grow[G_LB:G_LB + 2 * KT, :], lb_logits.rearrange("l (k p) -> (l k) p", p=P)),
                             (grow[G_Q:G_Q + 1, :], g_q_fox), (grow[G_K:G_K + 1, :], g_k_fox),
                             (grow[G_O:G_O + 1, :], g_o_hg)):
                pool.dma_start(dst, src).then_inc(const_in, 16)
            pool.wait_ge(const_set, 1)
            pool.dma_start(bf_c[P - H:P, :], b_f_fox.rearrange("a h -> h a")).then_inc(bias_in, 16)
            for i in range(2):
                pool.dma_start(pstage[i].rearrange("p (t n) -> p t n", t=TB),
                               p[i, 0].rearrange("(t p) n -> p t n", p=P)).then_inc(p_in, 16)

            def load_x(i):
                for j in range(4):
                    if not isinstance(i, int):
                        pool.wait_ge(x_turned, 4 * i + j - 3)
                    pool.dma_start(xstage[j].rearrange("p (t n) -> p t n", t=TB),
                                   x_tok[:, :, bass.ds((4 * i + j) * P, P)]).then_inc(x_in[j], 16)
            load_x(0)
            loop(pool, 1, KT // 4, load_x)

            def store_pe(i):
                for j in range(2):
                    pool.wait_ge(tile_out, 2 * i + j + 1)
                    pool.dma_start(pe_scr[2 * i + j], pe_tile[j]).then_inc(pe_stored[j], 16)
            loop(pool, 0, KT, store_pe)

            pool.wait_ge(f_cum, 1)
            pool.dma_start(c_scr, fc[P - H:P, :]).then_inc(c_stored, 16)
            pool.wait_ge(c_stored, 16)

            def decay_row(g):
                if not isinstance(g, int):
                    pool.wait_ge(negm_ready, TB * g)
                pool.dma_start(ckb, c_scr[bass.ds(g, 1), :].to_broadcast([P, S])).then_inc(ck_in, 16)
                pool.wait_ge(ck_in, 16 * g + 16)
                pool.tensor_tensor(ckm.rearrange("p (t n) -> p t n", t=TB),
                                   ckb.rearrange("p (t n) -> p t n", t=TB),
                                   causal[:, :].unsqueeze(1).to_broadcast([P, TB, P]),
                                   ALU.subtract).then_inc(ckm_ready, 1)
            pool.wait_ge(f_ln, 2)
            pool.wait_ge(cq_ready, 1)
            decay_row(0)
            loop(pool, 1, H, decay_row)

            for lay in range(2):
                def add_h(k, lay=lay):
                    pool.wait_ge(yn_ready, KT * lay + k + 1)
                    pool.tensor_tensor(hT[:, k], hT[:, k], yT[:, k], ALU.add).then_inc(hn_ready, 1)
                loop(pool, 0, KT, add_h)

                def load_pe(i, lay=lay):
                    for j in range(2):
                        if not isinstance(i, int):
                            pool.wait_ge(h_new, KT * lay + 2 * i + j - 1)
                        pool.dma_start(pe2[j], pe_scr[KT * lay + 2 * i + j]).then_inc(pe_in[j], 16)

                def store_out(i):
                    for j in range(2):
                        pool.wait_ge(out_staged, 2 * i + j + 1)
                        pool.dma_start(out_tok[:, :, bass.ds((2 * i + j) * P, P)],
                                       ostage2[j].rearrange("p (t n) -> p t n", t=TB)).then_inc(out_stored[j], 16)
                if lay == 0:
                    for j in range(2):
                        pool.wait_ge(pe_stored[j], 16 * KT)
                load_pe(0)
                if lay == 0:
                    loop(pool, 1, KT // 2, load_pe)
                else:
                    def turn(i):
                        load_pe(i)
                        store_out(i - 1)
                    loop(pool, 1, KT // 2, turn)
                    store_out(KT // 2 - 1)
            for j in range(2):
                pool.wait_ge(out_stored[j], 16 * KT // 2)

        @block.scalar
        def _(act):
            def split(u, i=0, per=0):
                n = u + per * i
                if isinstance(n, int) and n >= U_END:
                    return
                act.wait_ge(w_loaded[u % RAW], 16 * (u // RAW + 1) + (16 * per // RAW) * i)
                wait(act, w_used, n - RING + 1)
                act.activation(whi[:, u % RING].rearrange("p k n -> p (k n)"), raw[:, u % RAW, :],
                               ACT.Copy).then_inc(hi_done, 1)

            def split_x(stage, src, scale_at=None, ready=None, base=0):
                def one(k):
                    if ready is not None:
                        act.wait_ge(ready, base + k + 1)
                    scale = 1.0 if scale_at is None else gcol[:, bass.ds(scale_at + k, 1)]
                    act.activation(xhi[:, k], src[:, k], ACT.Copy, scale=scale).then_inc(xhi_done, 1)
                loop(act, 0, KT, one)

            def token_rms(stage):
                act.wait_ge(norm_done, stage + 1)
                act.activation(rinv[:, :], bank[7][:, :], ACT.Sqrt, bias=eps_c, scale=1.0 / D).then_inc(norm_rms, 1)

            for u in range(HI_AHEAD):
                split(u)
            act.wait_ge(g_turned, 1)
            act.activation(gcol[:, 0:G_ROWS], bank[7][:, 0:G_ROWS], ACT.Copy).then_inc(g_ready, 1)
            for n in range(2 * PK):
                act.wait_ge(pt_p, n + 1)
                act.activation(xhi[:, KT - 2 * PK + n], bank[2 + n][:, :], ACT.Copy).then_inc(phi_done, 1)
            act.wait_ge(p_ready, 2 * PK)

            def take_x(i):
                for j in range(4):
                    k = 4 * i + j
                    act.wait_ge(x_turned, k + 1)
                    act.activation(hT[:, k], bank[2 + j % 2][:, :], ACT.Copy).then_inc(h_ready, 1)
                    wait(act, acc_step, k - 1)
                    act.activation(sq2[j % 2], bank[2 + j % 2][:, :], ACT.Square).then_inc(sq_done, 1)
            take_x(0)
            loop(act, 1, KT // 4, take_x)
            act.wait_ge(lb_sem, 2)
            act.activation(lbc[:, 0:2], lbc[:, 0:2], ACT.Exp).then_inc(lb_exp, 1)

            def pe_units(i):
                for j in range(PE_UNITS):
                    split(U_PE + j + HI_AHEAD, i, PE_UNITS)
            loop(act, 0, 2, pe_units)
            act.wait_ge(w_used, U_F)
            act.wait_ge(h_ready, KT)
            split_x(0, hT, scale_at=G_PRE)
            for j in range(UPT):
                split(U_F + j + HI_AHEAD)
            token_rms(0)
            act.wait_ge(f_pre, 1)
            act.activation(fa[FR, :], fl[FR, :], ACT.Abs).then_inc(f_exp, 1)
            act.wait_ge(f_exp, 1)
            act.activation(fa[FR, :], fa[FR, :], ACT.Exp, scale=-1.0).then_inc(f_exp, 1)
            act.wait_ge(f_exp, 2)
            act.activation(fa[FR, :], fa[FR, :], ACT.Ln, bias=one_c[FR, :]).then_inc(f_ln, 1)

            def fox_head(h, proj=True, attn=True, first=False):
                g = h - 1
                for u in range(4 * UPT):
                    if proj:
                        split(U_FOX + u + HI_AHEAD, h, 4 * UPT)
                    if first and u == 4:
                        act.wait_ge(f_turned, 1)
                        act.activation(cq[:, :, :], bank[6][:, 0:TB * 32].rearrange("p (t n) -> p t n", t=TB),
                                       ACT.Copy).then_inc(cq_ready, 1)
                        for n in range(2):
                            act.wait_ge(pe_stored[n], 16 * KT)
                    if attn and u == 0:
                        act.wait_ge(stats_done, 2 * g + 1)
                        act.activation(sqq, bank[2][:, :], ACT.Sqrt, bias=eps_c, scale=1.0 / P).then_inc(rms_ready, 1)
                        act.wait_ge(stats_done, 2 * g + 2)
                        act.activation(sqk, bank[3][:, :], ACT.Sqrt, bias=eps_c, scale=1.0 / P).then_inc(rms_ready, 1)
                    if attn and u == 2:
                        act.wait_ge(vt_done, g + 1)
                        act.activation(vtok, bank[4][:, :], ACT.Copy).then_inc(vtok_ready, 1)
                        act.wait_ge(tile_out, T_FOX + 4 * g + 4)
                        act.activation(tz_t, z_t, ACT.Tanh).then_inc(tz_ready, 1)
                    if attn and u == 4:
                        for t in range(TB):
                            pr = prob[:, prob_at[t]:prob_at[t] + (t + 1) * P]
                            act.wait_ge(negm_ready, TB * g + t + 1)
                            act.activation(pr, pr, ACT.Exp, bias=negm[:, t:t + 1],
                                           accum_out=rsum[:, t:t + 1]).then_inc(exp_ready, 1)
                    if attn and u == 6:
                        act.wait_ge(pt_done, g + 1)
                        act.activation(probT[:, 0:512], bank[2][:, :], ACT.Copy)
                        act.activation(probT[:, 512:896], bank[3][:, 0:384], ACT.Copy)
                        act.activation(probT[:, 1152:1280], bank[3][:, 384:512], ACT.Copy)
                        act.activation(probT[:, 896:1152], bank[4][:, 0:256], ACT.Copy).then_inc(pt_ready, 1)
                    if proj and u == 4:
                        act.wait_ge(tile_out, T_FOX + 4 * h + 1)
                        act.activation(sqq, q_t, ACT.Square).then_inc(sq_ready, 1)
                    if proj and u == 5:
                        act.wait_ge(tile_out, T_FOX + 4 * h + 2)
                        act.activation(sqk, k_t, ACT.Square).then_inc(sq_ready, 1)

            def hg_head(h, proj=True, attn=True, first=False):
                g = h - 1
                for u in range(4 * UPT):
                    if proj:
                        split(U_HG + u + HI_AHEAD, h, 4 * UPT)
                    if first and u == 2:
                        token_rms(2)
                    if attn and u == 0:
                        act.wait_ge(hg_vt, g + 1)
                        act.activation(vtok, bank[4][:, :], ACT.Copy).then_inc(hg_vtok, 1)
                    if attn and u == 2:
                        act.wait_ge(tile_out, N_HG + 4 * g + 4)
                        act.activation(tz_t, z_t, ACT.Tanh).then_inc(hg_tz, 1)
                    if attn and u == 4:
                        act.wait_ge(kst_done, g + 1)
                        act.activation(kst[:, 0:3 * P], bank[4][:, 0:3 * P], ACT.Copy).then_inc(kst_ready, 1)
                    if proj and u == 5:
                        act.wait_ge(tile_out, N_HG + 4 * h + 2)
                        act.activation(f_t, f_t, ACT.Tanh, scale=0.5).then_inc(thf_ready, 1)
                    if attn and u == 5:
                        act.wait_ge(o_ready, g + 1)
                        act.activation(osq, o_t, ACT.Square).then_inc(osq_ready, 1)
                    if attn and u == 6:
                        act.wait_ge(ostat_done, g + 1)
                        act.activation(osq, bank[7][:, :], ACT.Sqrt, bias=eps_c, scale=1.0 / P).then_inc(orms_ready, 1)
                    if proj and u == 7:
                        act.wait_ge(tile_out, N_HG + 4 * h + 3)
                        act.activation(tq_t, q_t, ACT.Tanh).then_inc(tq_ready, 1)

            for lay, head in enumerate((fox_head, hg_head)):
                head(0, attn=False, first=True)
                loop(act, 1, H, head)
                head(H, proj=False)
                act.wait_ge(w_used, U_OUT[lay])
                split_x(3 * lay + 1, yT, ready=y_ready, base=KT * lay)

                def out_pair(i, lay=lay):
                    for j in range(2):
                        for m in range(UPT):
                            split(U_OUT[lay] + UPT * j + m + HI_AHEAD, i, 2 * UPT)
                        k = 2 * i + j
                        act.wait_ge(yo_ready, KT * lay + k + 1)
                        if not isinstance(i, int):
                            act.wait_ge(acc_step, KT * (2 * lay + 1) + k - 1)
                        act.activation(sq2[j], yT[:, k], ACT.Square).then_inc(sq_done, 1)
                out_pair(0)
                loop(act, 1, KT // 2, out_pair)
                token_rms(2 * lay + 1)
                split_x(3 * lay + 2, hT, ready=hn_ready, base=KT * lay)

                def gate_pair(i, lay=lay):
                    for j in range(2):
                        k = 2 * i + j
                        for m in range(UPT):
                            split(U_PG[lay] + UPT * j + m + HI_AHEAD, i, 2 * UPT)
                        act.wait_ge(w_used, U_PG[lay] + UPT * k + UPT)
                        if not isinstance(i, int):
                            act.wait_ge(h_new, KT * lay + k - 1)
                        act.activation(tg2[j], bank[T_PG[lay] % 2 ^ j][:, :], ACT.Tanh, scale=0.5).then_inc(tg_ready, 1)
                        if lay == 0:
                            act.wait_ge(h_new, k + 1)
                            if not isinstance(i, int):
                                act.wait_ge(acc_step, 2 * KT + k - 1)
                            act.activation(sq2[j], hT[:, k], ACT.Square).then_inc(sq_done, 1)
                        elif not (isinstance(k, int) and k == 0):
                            stage_out(k - 1, 1 - j)

                def stage_out(k, slot):
                    act.wait_ge(outT_done, k + 1)
                    if not isinstance(k, int):
                        if slot == 0:
                            act.wait_ge(out_stored[0], 8 * k)
                        else:
                            act.wait_ge(out_stored[1], 8 * k - 8)
                    elif k >= 2:
                        act.wait_ge(out_stored[slot], 16 * (k // 2))
                    act.activation(ostage2[slot], bank[2 + slot][:, :], ACT.Copy).then_inc(out_staged, 1)

                gate_pair(0)
                if lay == 0:
                    loop(act, 1, KT // 2, gate_pair)
                    act.wait_ge(w_used, U_HG)
                    split_x(3, hT, scale_at=G_PRE + KT)
                else:
                    gate_pair(1)
                    loop(act, 2, KT // 2 - 1, gate_pair)
                    gate_pair(KT // 2 - 1)
                    stage_out(KT - 1, 1)

        @block.vector
        def _(dve):
            steps = {"fixed": 0, "turn": None}

            def link(ins):
                ins.then_inc(v_step, 1)
                steps["fixed"] += 1
                turn = steps["turn"]
                dve.wait_ge(v_step, steps["fixed"] if turn is None else steps["fixed"] + turn)

            def linked_loop(first, last, links, body):
                start = steps["fixed"]
                with dve.Fori(first, last) as i:
                    steps["turn"] = links * (i - first)
                    body(i)
                    steps["turn"] = None
                assert steps["fixed"] == start + links, steps["fixed"] - start
                steps["fixed"] = start + links * (last - first)

            def split(u, i=0, per=0):
                n = u + per * i
                if isinstance(n, int) and n >= U_END:
                    return
                dve.wait_ge(hi_done, n + 1)
                wait(dve, w_used, n - RING + 1)
                dve.tensor_tensor(wlo[:, u % RING].rearrange("p k n -> p (k n)"), raw[:, u % RAW, :],
                                  whi[:, u % RING].rearrange("p k n -> p (k n)").bitcast(F32),
                                  ALU.subtract).then_inc(lo_done, 1)

            def split_x(stage, src, scale_at=None):
                def one(k):
                    dve.wait_ge(xhi_done, KT * stage + k + 1)
                    if scale_at is None:
                        dve.tensor_tensor(xlo[:, k], src[:, k], xhi[:, k].bitcast(F32),
                                          ALU.subtract).then_inc(x_ready, 1)
                    else:
                        dve.scalar_tensor_tensor(xlo[:, k], src[:, k], gcol[:, bass.ds(scale_at + k, 1)],
                                                 xhi[:, k].bitcast(F32), ALU.mult,
                                                 ALU.subtract).then_inc(x_ready, 1)
                loop(dve, 0, KT, one)

            def zero_acc():
                link(dve.memset(acc, 0.0))

            def add_square(k, stage, slot):
                dve.wait_ge(sq_done, KT * stage + k + 1)
                wait(dve, acc_step, KT * stage + k)
                dve.tensor_tensor(acc, acc, sq2[slot], ALU.add).then_inc(acc_step, 1)

            def token_rinv(stage):
                dve.wait_ge(norm_rms, stage + 1)
                dve.reciprocal(rinv[:, :], rinv[:, :]).then_inc(norm_ready, 1)
                dve.wait_ge(norm_ready, stage + 1)

            def take_tile(t0, used, dst, halve=False):
                dve.wait_ge(w_used, used)
                src = bank[t0 % 2][:, :]
                if halve:
                    dve.scalar_tensor_tensor(dst, src, 0.5, rinv[:, :], ALU.mult, ALU.mult).then_inc(tile_out, 1)
                else:
                    dve.tensor_tensor(dst, src, rinv[:, :], ALU.mult).then_inc(tile_out, 1)

            dve.memset(small[:, 2:3], 0.0)
            dve.memset(ones[:, :], 1.0).then_inc(const_set, 1)
            dve.memset(eps_c, EPS)
            dve.memset(one_c, 1.0)
            dve.memset(acc, 0.0)
            link(dve.memset(small[:, 3:4], 0.0))
            dve.wait_ge(const_in, 144)
            for t in range(TB):
                ins = dve.tensor_copy(levels[:, :, t * P // 2:(t + 1) * P // 2],
                                      level_in.rearrange("p (l n) -> p l n", l=LEVELS))
            link(ins)
            for u in range(LO_AHEAD):
                split(u)
            for n in range(2 * PK):
                dve.wait_ge(phi_done, n + 1)
                dve.tensor_tensor(xlo[:, KT - 2 * PK + n], bank[2 + n][:, :],
                                  xhi[:, KT - 2 * PK + n].bitcast(F32), ALU.subtract).then_inc(p_ready, 1)
            dve.wait_ge(g_ready, 1)
            link(dve.tensor_scalar(gcol[:, G_Q:G_Q + 1], gcol[:, G_Q:G_Q + 1], float(P) ** -0.5, None, ALU.mult))
            l0, l1 = gcol[:, G_LB:G_LB + KT], gcol[:, G_LB + KT:G_LB + 2 * KT]
            link(dve.tensor_tensor(lbc[:, 2], l0, l1, ALU.max))
            dve.tensor_tensor(lbc[:, 0], l0, lbc[:, 2], ALU.subtract).then_inc(lb_sem, 1)
            dve.tensor_tensor(lbc[:, 1], l1, lbc[:, 2], ALU.subtract).then_inc(lb_sem, 1)

            def take_squares(i):
                for j in range(4):
                    add_square(4 * i + j, 0, j % 2)
            take_squares(0)
            loop(dve, 1, KT // 4, take_squares)
            dve.wait_ge(lb_exp, 1)
            link(dve.tensor_tensor(lbc[:, 2], lbc[:, 0], lbc[:, 1], ALU.add))
            link(dve.reciprocal(lbc[:, 2], lbc[:, 2]))
            dve.tensor_tensor(lbc[:, 3], lbc[:, 0], lbc[:, 2], ALU.mult)
            link(dve.tensor_tensor(lbc[:, 5], lbc[:, 1], lbc[:, 2], ALU.mult))
            link(dve.tensor_tensor(lbc[:, 4], lbc[:, 3], lbc[:, 5], ALU.add))
            link(dve.tensor_tensor(lbc[:, 4], lbc[:, 4], lbc[:, 3], ALU.subtract))
            link(dve.tensor_scalar(lbc[:, 5], lbc[:, 4], -1.0, 1.0, ALU.mult, ALU.add))
            lower, upper = lbc[:, 4], lbc[:, 5]

            def pe_units(i):
                for j in range(PE_UNITS):
                    split(U_PE + j + LO_AHEAD, i, PE_UNITS)
                    for f in range(4):
                        n = 4 * j + f
                        if f < 3:
                            dve.wait_ge(embed_done, 3 * (PE_UNITS * i + j) + f + 1)
                        else:
                            dve.wait_ge(w_used, PE_UNITS * i + j + 1)
                        wait(dve, pe_stored[n % 2], (KT // 2) * 16 * i + 16 * (n // 2))
                        dve.tensor_copy(pe_tile[n % 2], bank[n % 2][:, :]).then_inc(tile_out, 1)
            pe_units(0)
            pe_units(1)
            split_x(0, hT, scale_at=G_PRE)
            for j in range(UPT):
                split(U_F + j + LO_AHEAD)
            token_rinv(0)
            link(dve.memset(fone, 1.0))
            dve.wait_ge(w_used, U_F + UPT)
            dve.tensor_tensor(fl[FR, :], bank[T_F % 2][FR, :], rinv[FR, :], ALU.mult).then_inc(tile_out, 1)
            dve.wait_ge(tile_out, T_F + 1)
            dve.wait_ge(bias_in, 16)
            dve.tensor_scalar(fl[FR, :], fl[FR, :], bf_c[FR, :], None, ALU.add).then_inc(f_pre, 1)
            dve.wait_ge(f_ln, 1)
            dve.scalar_tensor_tensor(fl[FR, :], fl[FR, :], 0.0, fa[FR, :], ALU.min, ALU.subtract).then_inc(f_ln, 1)
            dve.wait_ge(f_ln, 2)
            dve.tensor_tensor_scan(fc[FR, :], fone[FR, :], fl[FR, :], 0.0, ALU.mult, ALU.add).then_inc(f_cum, 1)

            def fox_head(h, proj=True, attn=True):
                g = h - 1
                for u in range(4 * UPT):
                    if proj:
                        split(U_FOX + u + LO_AHEAD, h, 4 * UPT)
                    if attn and u == 0:
                        take_tile(T_FOX + 3, U_FOX + 4 * UPT * g + 4 * UPT, z_t, halve=True)
                    if attn and u in (0, 1):
                        r, t, gc = ((sqq, q_t, G_Q), (sqk, k_t, G_K))[u]
                        dve.wait_ge(rms_ready, 2 * g + u + 1)
                        link(dve.reciprocal(r, r))
                        dve.scalar_tensor_tensor(t, t, gcol[:, gc:gc + 1], r, ALU.mult, ALU.mult).then_inc(qk_ready, 1)
                    if attn and u == 2:
                        dve.wait_ge(tz_ready, g + 1)
                        dve.scalar_tensor_tensor(tz_t, tz_t, 1.0, z_t, ALU.add, ALU.mult).then_inc(zs_ready, 1)
                    if attn and u == 3:
                        dve.wait_ge(scores_done, g + 1)
                    if proj and u == 3:
                        take_tile(T_FOX, U_FOX + 4 * UPT * h + 1 * UPT, q_t)
                    if attn and u == 3:
                        dve.wait_ge(ckm_ready, g + 1)
                        for t in range(TB):
                            at, n = prob_at[t], t * P
                            src = score_of(t)
                            c_query = cq[:, t, bass.ds(32 - H + g, 1)]
                            if t:
                                dve.scalar_tensor_tensor(prob[:, at:at + n], src[:, 0:n], c_query, ckb[:, 0:n],
                                                         ALU.add, ALU.subtract)
                            ins = dve.scalar_tensor_tensor(prob[:, at + n:at + n + P], src[:, n:n + P], c_query,
                                                           ckm[:, n:n + P], ALU.add, ALU.subtract)
                        link(ins)
                        for t in range(TB):
                            dve.tensor_reduce(negm[:, t:t + 1], prob[:, prob_at[t]:prob_at[t] + (t + 1) * P],
                                              AX.X, ALU.max, negate=True).then_inc(negm_ready, 1)
                    if proj and u == 4:
                        take_tile(T_FOX + 1, U_FOX + 4 * UPT * h + 2 * UPT, k_t)
                    if attn and u == 5:
                        dve.wait_ge(exp_ready, TB * g + TB)
                        link(dve.reciprocal(rsum, rsum))
                        for t in range(TB):
                            pr = prob[:, prob_at[t]:prob_at[t] + (t + 1) * P]
                            ins = dve.tensor_scalar(pr, pr, rsum[:, t:t + 1], None, ALU.mult)
                        ins.then_inc(probs_ready, 1)
                    if proj and u == 6:
                        take_tile(T_FOX + 2, U_FOX + 4 * UPT * h + 3 * UPT, v_t)
                    if attn and u == 7:
                        dve.wait_ge(pv_done, g + 1)
                        dve.wait_ge(zs_ready, g + 1)
                        dve.tensor_tensor(yT[:, g], bank[5][:, :], tz_t, ALU.mult).then_inc(y_ready, 1)

            def score_of(t):
                return {0: bank[6][:, 384:512], 1: bank[7][:, 0:256], 2: bank[6][:, 0:384], 3: bank[5][:, :]}[t]

            def pairs(tile, n):
                return tile.rearrange("p (b e n) -> p b e n", e=2, n=n)

            def tree_of(lv):
                if lv == 0:
                    return f_t
                at = S - (S >> (lv - 1))
                return tree[:, at:at + (S >> lv)]

            def hg_head(h, proj=True, attn=True, first=False):
                g = h - 1

                def level(lv):
                    n = 1 << lv
                    dve.wait_ge(level_done, LEVELS * g + lv + 1)
                    dve.wait_ge(level_ready, (LEVELS + 1) * g + lv + 1)
                    if lv:
                        dve.wait_ge(att_ready, LEVELS * g + lv)
                    t = tree_of(lv).rearrange("p (b e) -> p b e", e=2)
                    qh, kh = pairs(q_t, n)[:, :, 1], pairs(k_t, n)[:, :, 0]
                    nb = S // (2 * n)
                    dve.tensor_tensor(qh, qh, t[:, :, 0:1].to_broadcast([P, nb, n]), ALU.mult)
                    dve.tensor_tensor(kh, kh, t[:, :, 1:2].to_broadcast([P, nb, n]), ALU.mult)
                    dve.tensor_tensor(tree_of(lv + 1), t[:, :, 0], t[:, :, 1], ALU.mult).then_inc(level_ready, 1)
                    dve.copy_predicated(pairs(att, n)[:, :, 1],
                                        levels[:, lv].rearrange("p (b n) -> p b n", n=n),
                                        bank[2 + lv % 2][:, 0:S // 2].rearrange("p (b n) -> p b n", n=n)
                                        ).then_inc(att_ready, 1)

                for u in range(4 * UPT):
                    if attn and u == 0:
                        dve.wait_ge(diag_done, g + 1)
                        dve.tensor_tensor(att.rearrange("p (t n) -> p t n", t=TB),
                                          bank[5][:, :].rearrange("p (t n) -> p t n", t=TB),
                                          ident[:, :].unsqueeze(1).to_broadcast([P, TB, P]), ALU.mult)
                        dve.tensor_tensor(q_t, q_t, f_t, ALU.mult).then_inc(level_ready, 1)
                    if attn and 1 <= u < 4:
                        level(2 * u - 1)
                    if proj:
                        split(U_HG + u + LO_AHEAD, h, 4 * UPT)
                    if attn and u < 4:
                        level(2 * u)
                    if attn and u == 0:
                        take_tile(T_HG + 3, U_HG + 4 * UPT * g + 4 * UPT, z_t, halve=True)
                    if first and u == 2:
                        token_rinv(2)
                    if proj and u == 2:
                        if attn:
                            dve.wait_ge(hg_vt, g + 1)
                        take_tile(T_HG, U_HG + 4 * UPT * h + 1 * UPT, v_t)
                    if proj and u == 4:
                        take_tile(T_HG + 1, U_HG + 4 * UPT * h + 2 * UPT, f_t)
                    if attn and u == 4:
                        dve.wait_ge(u_done, g + 1)
                        dve.wait_ge(level_ready, (LEVELS + 1) * (g + 1))
                        total = tree_of(LEVELS)
                        link(dve.tensor_copy(st[:, 0:P], bank[5][:, 0:P]))
                        link(dve.scalar_tensor_tensor(st[:, P:2 * P], st[:, 0:P], total[:, 1:2],
                                                      bank[5][:, P:2 * P], ALU.mult, ALU.add))
                        dve.scalar_tensor_tensor(st[:, 2 * P:3 * P], st[:, P:2 * P], total[:, 2:3],
                                                 bank[5][:, 2 * P:3 * P], ALU.mult, ALU.add).then_inc(state_ready, 1)
                    if attn and u == 5:
                        dve.wait_ge(ot_done, g + 1)
                        dve.tensor_copy(o_t, bank[6][:, :]).then_inc(o_ready, 1)
                    if proj and u == 5:
                        dve.wait_ge(thf_ready, h + 1)
                        link(dve.tensor_scalar(f_t, f_t, 0.5, 0.5, ALU.mult, ALU.add))
                        link(dve.tensor_scalar(f_t, f_t, upper[:, bass.ds(h, 1)], lower[:, bass.ds(h, 1)],
                                               ALU.mult, ALU.add))
                        dve.tensor_scalar(k_t, f_t, -1.0, 1.0, ALU.mult, ALU.add)
                    if proj and u == 6:
                        take_tile(T_HG + 2, U_HG + 4 * UPT * h + 3 * UPT, q_t, halve=True)
                    if attn and u == 6:
                        dve.wait_ge(orms_ready, g + 1)
                        link(dve.reciprocal(osq, osq))
                        dve.wait_ge(o_ready, g + 1)
                        dve.scalar_tensor_tensor(o_t, o_t, gcol[:, G_O:G_O + 1], osq, ALU.mult, ALU.mult)
                    if proj and u == 7:
                        dve.wait_ge(tq_ready, h + 1)
                        dve.wait_ge(tile_out, N_HG + 4 * h + 3)
                        dve.scalar_tensor_tensor(q_t, tq_t, 1.0, q_t, ALU.add, ALU.mult).then_inc(hg_qk, 1)
                    if attn and u == 7:
                        dve.wait_ge(hg_tz, g + 1)
                        link(dve.scalar_tensor_tensor(tz_t, tz_t, 1.0, z_t, ALU.add, ALU.mult))
                        dve.tensor_tensor(yT[:, g], o_t, tz_t, ALU.mult).then_inc(y_ready, 1)

            for lay, (head, links) in enumerate(((fox_head, 4), (hg_head, 6))):
                if lay:
                    head(0, attn=False, first=True)
                else:
                    head(0, attn=False)
                linked_loop(1, H, links, head)
                head(H, proj=False)
                split_x(3 * lay + 1, yT)
                zero_acc()

                def out_pair(i, lay=lay):
                    for j in range(2):
                        k = 2 * i + j
                        for m in range(UPT):
                            split(U_OUT[lay] + UPT * j + m + LO_AHEAD, i, 2 * UPT)
                        dve.wait_ge(w_used, U_OUT[lay] + UPT * k + UPT)
                        dve.tensor_copy(yT[:, k], bank[T_OUT[lay] % 2 ^ j][:, :]).then_inc(yo_ready, 1)
                        add_square(k, 2 * lay + 1, j)
                out_pair(0)
                loop(dve, 1, KT // 2, out_pair)
                token_rinv(2 * lay + 1)

                def scale_y(k, lay=lay):
                    dve.scalar_tensor_tensor(yT[:, k], yT[:, k], gcol[:, bass.ds(G_POST + KT * lay + k, 1)],
                                             rinv[:, :], ALU.mult, ALU.mult).then_inc(yn_ready, 1)
                loop(dve, 0, KT, scale_y)
                split_x(3 * lay + 2, hT)
                if lay == 0:
                    zero_acc()

                def gate_pair(i, lay=lay):
                    for j in range(2):
                        k = 2 * i + j
                        for m in range(UPT):
                            split(U_PG[lay] + UPT * j + m + LO_AHEAD, i, 2 * UPT)
                        dve.wait_ge(tg_ready, KT * lay + k + 1)
                        dve.wait_ge(pe_in[j], 16 * (KT // 2) * lay + 16 * i + 16)
                        link(dve.scalar_tensor_tensor(tg2[j], tg2[j], 1.0, pe2[j], ALU.add, ALU.mult))
                        if lay and not isinstance(i, int):
                            dve.wait_ge(outT_done, k - 1)
                        dst = hout2[j] if lay else hT[:, k]
                        dve.scalar_tensor_tensor(dst, tg2[j], 0.5, hT[:, k], ALU.mult, ALU.add).then_inc(h_new, 1)
                        if lay == 0:
                            add_square(k, 2, j)
                gate_pair(0)
                if lay == 0:
                    linked_loop(1, KT // 2, 2, gate_pair)
                    split_x(3, hT, scale_at=G_PRE + KT)
                else:
                    linked_loop(1, KT // 2 - 1, 2, gate_pair)
                    dve.wait_ge(outT_done, KT - 2)
                    gate_pair(KT // 2 - 1)

        @block.tensor
        def _(pe):
            def product(dst, u, b, k, first, last):
                hi, lo = whi[:, u % RING, b], wlo[:, u % RING, b]
                pe.matmul(dst, hi, xhi[:, k], start=first, stop=False)
                pe.matmul(dst, hi, xlo[:, k], start=False, stop=False)
                return pe.matmul(dst, lo, xhi[:, k], start=False, stop=last)

            def unit(u, i, per, t0, t, half, freed=tile_out, stage=None, mid=None):
                pe.wait_ge(lo_done, u + per * i + 1)
                if half == 0:
                    wait(pe, freed, t - 1)
                for b in range(UB):
                    k = UB * half + b
                    if stage is not None:
                        pe.wait_ge(x_ready, KT * stage + k + 1)
                    ins = product(bank[t0 % 2][:, :], u, b, k, k == 0, k == KT - 1)
                    if b == UB // 2 - 1 and mid is not None:
                        mid()
                ins.then_inc(w_used, 1)

            def turn(dst, src, n, ins=None):
                for t in range(n):
                    ins = pe.transpose(dst[:, t * P:(t + 1) * P], src[:, t * P:(t + 1) * P], ident[:, :])
                return ins

            def sum_squares(stage):
                pe.wait_ge(acc_step, KT * (stage + 1))
                pe.matmul(bank[7][:, :], ones[:, :], acc, start=True, stop=True).then_inc(norm_done, 1)

            pe.wait_ge(const_in, 144)
            pe.transpose(bank[7][:, 0:G_ROWS], grow[0:G_ROWS, :], ident[0:G_ROWS, 0:G_ROWS]).then_inc(g_turned, 1)
            pe.wait_ge(p_in, 32)
            for i in range(2):
                for k in range(PK):
                    for t in range(TB):
                        at = t * PLE + k * P
                        ins = pe.transpose(bank[2 + PK * i + k][:, t * P:(t + 1) * P],
                                           pstage[i][:, at:at + P], ident[:, :])
                    ins.then_inc(pt_p, 1)
            pe.wait_ge(p_ready, 2 * PK)

            def turn_x(i):
                for j in range(4):
                    k = 4 * i + j
                    pe.wait_ge(x_in[j], 16 * i + 16)
                    wait(pe, sq_done, k - 1)
                    turn(bank[2 + j % 2], xstage[j], TB).then_inc(x_turned, 1)
            turn_x(0)
            loop(pe, 1, KT // 4, turn_x)

            def embed(i):
                for j in range(PE_UNITS):
                    u = U_PE + j
                    pe.wait_ge(lo_done, u + PE_UNITS * i + 1)
                    for f in range(4):
                        n = 4 * j + f
                        wait(pe, tile_out, KT * i + n - 1)
                        for k in range(PK):
                            at = KT - 2 * PK + PK * i + k
                            ins = product(bank[n % 2][:, :], u, 4 * k + f, at, k == 0, k == PK - 1)
                        ins.then_inc(embed_done if f < 3 else w_used, 1)
            embed(0)
            embed(1)
            for half in range(UPT):
                unit(U_F + half, 0, 0, T_F, T_F, half, stage=0)
            sum_squares(0)
            def turn_c():
                pe.wait_ge(f_cum, 1)
                for t in range(TB):
                    ins = pe.transpose(bank[6][:, 32 * t:32 * (t + 1)], fc[FR, t * P:(t + 1) * P], ident[FR, FR])
                ins.then_inc(f_turned, 1)

            def fox_head(h, proj=True, attn=True, first=False):
                g = h - 1
                for u in range(4 * UPT):
                    if attn and u == 0:
                        pe.wait_ge(tile_out, T_FOX + 4 * g + 3)
                        turn(bank[4], v_t, TB).then_inc(vt_done, 1)
                        for n, sq in enumerate((sqq, sqk)):
                            pe.wait_ge(sq_ready, 2 * g + n + 1)
                            pe.matmul(bank[2 + n][:, :], ones[:, :], sq, start=True, stop=True).then_inc(stats_done, 1)
                    if proj:
                        j = u // UPT
                        unit(U_FOX + u, h, 4 * UPT, T_FOX + j, T_FOX + 4 * h + j, u % UPT)
                    if first and u == 3:
                        turn_c()
                    if attn and u == 2:
                        pe.wait_ge(qk_ready, 2 * g + 2)
                        pe.wait_ge(tile_out, T_FOX + 4 * g + 4)
                        for t in range(TB):
                            n = (t + 1) * P
                            dst = {0: bank[6][:, 384:512], 1: bank[7][:, 0:256],
                                   2: bank[6][:, 0:384], 3: bank[5][:, :]}[t]
                            ins = pe.matmul(dst, q_t[:, t * P:n], k_t[:, 0:n], start=True, stop=True)
                        ins.then_inc(scores_done, 1)
                    if attn and u == 5:
                        pe.wait_ge(probs_ready, g + 1)
                        pe.wait_ge(vtok_ready, g + 1)
                        dsts = [bank[2][:, :], bank[3][:, 0:384], bank[4][:, 0:256], bank[3][:, 384:512]]
                        for kb in range(TB):
                            for t in range(kb, TB):
                                at = prob_at[t] + kb * P
                                ins = pe.transpose(dsts[kb][:, (t - kb) * P:(t - kb + 1) * P],
                                                   prob[:, at:at + P], ident[:, :])
                        ins.then_inc(pt_done, 1)
                    if attn and u == 6:
                        pe.wait_ge(pt_ready, g + 1)
                        for kb in range(TB):
                            n = S - kb * P
                            ins = pe.matmul(bank[5][:, kb * P:S], vtok[:, kb * P:(kb + 1) * P],
                                            probT[:, probT_at[kb]:probT_at[kb] + n],
                                            start=(kb == 0), stop=(kb == TB - 1))
                        ins.then_inc(pv_done, 1)

            def hg_head(h, proj=True, attn=True, first=False):
                g = h - 1

                def level(lv):
                    n = 1 << lv
                    pe.wait_ge(level_ready, (LEVELS + 1) * g + lv + 1)
                    if lv >= 2:
                        pe.wait_ge(att_ready, LEVELS * g + lv - 1)
                    for t in range(TB):
                        rhs = q_t[:, t * P:(t + 1) * P].rearrange("p (b e n) -> p b e n", e=2, n=n)[:, :, 1]
                        dst = bank[2 + lv % 2][:, t * P // 2:(t + 1) * P // 2].rearrange("p (b n) -> p b n", n=n)
                        ins = pe.matmul(dst, k_t[:, t * P:(t + 1) * P], rhs, start=True, stop=True)
                    ins.then_inc(level_done, 1)

                def slot(n):
                    if n == 0:
                        pe.wait_ge(tile_out, N_HG + 4 * g + 1)
                        turn(bank[4], v_t, TB).then_inc(hg_vt, 1)
                        pe.wait_ge(hg_qk, g + 1)
                        for t in range(TB):
                            c = slice(t * P, (t + 1) * P)
                            ins = pe.matmul(bank[5][:, c], k_t[:, c], q_t[:, c], start=True, stop=True)
                        ins.then_inc(diag_done, 1)
                    if 1 <= n <= LEVELS:
                        level(n - 1)
                    if n == 8:
                        pe.wait_ge(level_ready, (LEVELS + 1) * (g + 1))
                        pe.wait_ge(hg_vtok, g + 1)
                        turn(bank[4], k_t, TB - 1).then_inc(kst_done, 1)
                    if n == 9:
                        pe.wait_ge(kst_ready, g + 1)
                        for t in range(TB - 1):
                            c = slice(t * P, (t + 1) * P)
                            ins = pe.matmul(bank[5][:, c], kst[:, c], vtok[:, c], start=True, stop=True)
                        ins.then_inc(u_done, 1)
                    if n == 10:
                        pe.wait_ge(state_ready, g + 1)
                        pe.wait_ge(att_ready, LEVELS * (g + 1))
                        for t in range(TB):
                            c = slice(t * P, (t + 1) * P)
                            ins = pe.matmul(bank[6][:, c], vtok[:, c], att[:, c], start=True, stop=(t == 0))
                            if t:
                                ins = pe.matmul(bank[6][:, c], st[:, (t - 1) * P:t * P], q_t[:, c],
                                                start=False, stop=True)
                        ins.then_inc(ot_done, 1)
                    if n == 12:
                        pe.wait_ge(osq_ready, g + 1)
                        pe.matmul(bank[7][:, :], ones[:, :], osq, start=True, stop=True).then_inc(ostat_done, 1)

                for u in range(4 * UPT):
                    if attn:
                        slot(2 * u)
                    if proj:
                        j = u // UPT
                        unit(U_HG + u, h, 4 * UPT, T_HG + j, N_HG + 4 * h + j, u % UPT,
                             stage=3 if first and j == 0 else None,
                             mid=(lambda u=u: slot(2 * u + 1)) if attn else None)
                    elif attn:
                        slot(2 * u + 1)
                    if first and u == 1:
                        sum_squares(2)

            for lay, head in enumerate((fox_head, hg_head)):
                head(0, attn=False, first=True)
                loop(pe, 1, H, head)
                head(H, proj=False)

                def out_pair(i, lay=lay):
                    for j in range(2):
                        for half in range(UPT):
                            unit(U_OUT[lay] + UPT * j + half, i, 2 * UPT, T_OUT[lay] + j,
                                 2 * i + j + KT * lay, half, freed=yo_ready,
                                 stage=3 * lay + 1 if isinstance(i, int) and j == 0 else None)
                out_pair(0)
                loop(pe, 1, KT // 2, out_pair)
                sum_squares(2 * lay + 1)

                def gate_pair(i, lay=lay):
                    for j in range(2):
                        k = 2 * i + j
                        for half in range(UPT):
                            unit(U_PG[lay] + UPT * j + half, i, 2 * UPT, T_PG[lay] + j,
                                 k + KT * lay, half, freed=tg_ready,
                                 stage=3 * lay + 2 if isinstance(i, int) and i == 0 and j == 0 else None)
                            if lay and half == 0 and not (isinstance(k, int) and k == 0):
                                turn_out(k - 1, 1 - j)

                def turn_out(k, slot):
                    pe.wait_ge(h_new, KT + k + 1)
                    wait(pe, out_staged, k - 1)
                    turn(bank[2 + slot], hout2[slot], TB).then_inc(outT_done, 1)
                gate_pair(0)
                if lay == 0:
                    loop(pe, 1, KT // 2, gate_pair)
                else:
                    gate_pair(1)
                    loop(pe, 2, KT // 2, gate_pair)
                    turn_out(KT - 1, 1)


_INS = ["x", "p", "w_in_fox", "b_f_fox", "g_q_fox", "g_k_fox", "w_out_fox", "w_in_hg", "lb_logits", "g_o_hg",
        "w_out_hg", "pre_norm", "post_norm", "w_pe", "w_pg"]


def kernel(**inputs):
    import numpy as _np
    import concourse.bacc as _bacc
    from concourse import mybir as _mybir
    from concourse.bass_utils import run_bass_kernel_spmd as _run

    ident = _np.eye(P, dtype=_np.float32)
    causal = _np.where(_np.arange(P)[None, :] <= _np.arange(P)[:, None], 0.0, NEG).astype(_np.float32)
    levels = _np.zeros((P, LEVELS, P // 2), _np.float32)
    for lv in range(LEVELS):
        n = 1 << lv
        s = _np.arange(P)
        b = _np.arange(P // 2) // n
        levels[:, lv, :] = (s[:, None] // (2 * n) == b[None, :]) & (s[:, None] % (2 * n) < n)
    consts = {"c_ident": ident, "c_causal": causal, "c_levels": levels.reshape(P, -1)}

    nc = _bacc.Bacc("TRN2", target_bir_lowering=False, num_devices=1)
    arrays, args = {}, []
    for name in _INS + list(consts):
        a = consts[name] if name in consts else _np.ascontiguousarray(inputs[name])
        arrays[f"in_{name}_dram"] = a
        args.append(nc.dram_tensor(f"in_{name}_dram", a.shape, _mybir.dt.from_np(a.dtype), kind="ExternalInput").ap())
    args.append(nc.dram_tensor("out_0_dram", (1, S, D), _mybir.dt.float32, kind="ExternalOutput").ap())
    trunk(nc, *args)
    r = _run(nc, [arrays], core_ids=[0])
    return r.results[0]["out_0_dram"]
```

```python
from contextlib import ExitStack

import concourse.bass as bass
from concourse import mybir

F32 = mybir.dt.float32
F32R = mybir.dt.float32r
U8 = mybir.dt.uint8
ALU = mybir.AluOpType
ACT = mybir.ActivationFunctionType
AX = mybir.AxisListType

P = 128
S = 512
D = 2048
KT = D // P
TB = S // P
H = D // P
PLE = 256
PK = PLE // P
EPS = 1e-6
NEG = -1e30
LEVELS = 7

UB = 8
UPT = KT // UB
PE_UNITS = PK * KT // UB
RAW, RING = 2, 4
NORM_LAG = 3
GATE_BANKS = [4, 5]
HI_AHEAD, LO_AHEAD = 3, 2
U_PE = 0
U_F = U_PE + 2 * PE_UNITS
U_FOX = U_F + UPT
U_OUT = [U_FOX + 4 * UPT * H, 0]
U_PG = [U_OUT[0] + UPT * KT, 0]
U_HG = U_PG[0] + UPT * KT
U_OUT[1] = U_HG + 4 * UPT * H
U_PG[1] = U_OUT[1] + UPT * KT
U_END = U_PG[1] + UPT * KT

T_PE = 0
T_F = T_PE + 2 * KT
T_FOX = T_F + 1
T_OUT = [T_FOX + 4 * H, 0]
T_PG = [T_OUT[0] + KT, 0]
T_HG = T_PG[0] + KT
T_OUT[1] = T_HG + 4 * H
T_PG[1] = T_OUT[1] + KT
N_HG = T_FOX + 4 * H

FOX_FILL = {0: [(0, 0, 8)], 1: [(1, 0, 4)], 3: [(1, 4, 8)], 4: [(2, 0, 7)], 5: [(3, 0, 2)], 6: [(3, 2, 5)],
            7: [(3, 5, 7)]}
HG_FILL = {0: [(0, 0, 3)], 1: [(0, 3, 5)], 2: [(0, 5, 7)], 3: [(0, 7, 8), (1, 0, 1)], 4: [(1, 1, 3)], 5: [(1, 3, 5)],
           6: [(1, 5, 7)], 7: [(1, 7, 8), (2, 0, 1)], 8: [(2, 1, 3)], 9: [(2, 3, 6)], 10: [(2, 6, 7), (3, 0, 2)],
           12: [(3, 2, 7)]}
FOX_HI = {0: (0, 2, []), 1: (2, 8, [3]), 2: (8, 15, []), 3: (0, 0, [4]), 5: (0, 0, [5])}
FOX_LO = {3: [2], 4: [3], 6: [4], 7: [5]}
HG_HI = {0: (0, 6, []), 1: (6, 10, [3]), 2: (10, 15, []), 3: (0, 0, [4]), 5: (0, 0, [5])}
HG_LO = {1: [2], 2: [3], 4: [4], 5: [5]}

G_PRE, G_POST, G_LB, G_Q, G_K, G_O, G_ROWS = 0, 2 * KT, 4 * KT, 6 * KT, 6 * KT + 1, 6 * KT + 2, 6 * KT + 3


def trunk(nc, x, p, w_in_fox, b_f_fox, g_q_fox, g_k_fox, w_out_fox, w_in_hg, lb_logits, g_o_hg,
          w_out_hg, pre_norm, post_norm, w_pe, w_pg, c_ident, c_causal, c_levels, out):
    pe_scr = nc.dram_tensor("pe_scr", (2 * KT, P, S), F32, kind="Internal").ap()
    c_scr = nc.dram_tensor("c_scr", (H, S), F32, kind="Internal").ap()

    def rows_of(w):
        return w.rearrange("(k p) n -> p k n", p=P)

    wf, wh = rows_of(w_in_fox[0]), rows_of(w_in_hg[0])
    wo = [rows_of(w_out_fox[0]), rows_of(w_out_hg[0])]
    wg = [rows_of(w_pg[i]) for i in range(2)]
    x_tok = x[0].rearrange("(t p) n -> p t n", p=P)
    out_tok = out[0].rearrange("(t p) n -> p t n", p=P)

    ctx = ExitStack()
    with ctx:
        def sb(name, shape, dt=F32):
            return ctx.enter_context(nc.sbuf_tensor(name, shape, dt))

        def sem(name):
            return ctx.enter_context(nc.semaphore(name))

        ctx.enter_context(nc.allow_non_contiguous_dma(reason="one column of forget biases"))

        hT = sb("hT", [P, KT, S])
        xhi = sb("xhi", [P, KT, S], F32R)
        xlo = sb("xlo", [P, KT, S], F32R)
        yT = sb("yT", [P, KT, S])
        raw = sb("raw", [P, RAW, UB * P])
        whi = sb("whi", [P, RING, UB, P], F32R)
        wlo = sb("wlo", [P, RING, UB, P], F32R)
        rinv = sb("rinv", [P, S])
        ident = sb("ident", [P, P])
        ones = sb("ones", [P, P])
        kmix = sb("kmix", [P, TB // 2, P])
        causal = sb("causal", [P, P])
        levels = sb("levels", [P, LEVELS, S // 2], U8)
        gcol = sb("gcol", [P, P])
        lbc = sb("lbc", [P, 6, KT])
        cq = sb("cq", [P, TB, 32])
        small = sb("small", [P, 16])
        eps_c, one_c, bf_c = small[:, 0:1], small[:, 1:2], small[:, 2:3]
        negm, rsum = small[:, 4:8], small[:, 8:12]
        work = sb("work", [P, 15 * S])

        def wk(i, n=1):
            return work[:, i * S:(i + n) * S]

        q_t, k_t, v_t, z_t, tz_t, vtok = wk(0), wk(1), wk(2), wk(3), wk(4), wk(14)
        sqq, sqk, ckb, ckm = wk(5), wk(6), wk(7), wk(8)
        prob, probT = work[:, 9 * S:9 * S + 1280], work[:, 9 * S + 1280:9 * S + 2560]
        prob_at = [0, 128, 384, 768]
        probT_at = [0, 512, 896, 1152]
        osq, f_t, tree, att, kst, st, o_t, tq_t = (wk(i) for i in range(5, 13))
        sq2, acc = [wk(5), wk(6)], wk(13)
        tg2, pe2, hout2, ostage2 = [wk(0), wk(1)], [wk(2), wk(3)], [wk(7), wk(8)], [wk(9), wk(10)]
        xstage = [wk(i) for i in range(4)]
        pstage = [wk(7, 2), wk(9, 2)]
        pe_tile = [wk(12), wk(4), wk(14), wk(7)]
        embed_banks = [0, 1, 4, 5]
        grow, level_in = yT[:, 0, 0:P], yT[:, 1:3].rearrange("p a n -> p (a n)")[:, 0:LEVELS * P]
        fl, fa, fc, fone = wk(7), wk(8), wk(9), wk(10)
        FR = slice(P - 32, P)

        bank = [ctx.enter_context(nc.psum_tensor(f"bank{i}", [P, S], F32)) for i in range(8)]

        w_loaded = [sem(f"w_loaded{i}") for i in range(RAW)]
        hi_done, lo_done, w_used = sem("hi_done"), sem("lo_done"), sem("w_used")
        embed_done, tile_out = sem("embed_done"), sem("tile_out")
        xhi_done, x_ready = sem("xhi_done"), sem("x_ready")
        acc_zero, sq_done, acc_step = sem("acc_zero"), sem("sq_done"), sem("acc_step")
        norm_done, norm_rms, norm_ready = sem("norm_done"), sem("norm_rms"), sem("norm_ready")
        y_ready, yo_ready, yn_ready, hn_ready = sem("y_ready"), sem("yo_ready"), sem("yn_ready"), sem("hn_ready")
        tg_ready, h_new = sem("tg_ready"), sem("h_new")
        gvec_in, const_in, const_set, bias_in = sem("gvec_in"), sem("const_in"), sem("const_set"), sem("bias_in")
        p_in = [sem("p_in0"), sem("p_in1")]
        pt_p, phi_done, p_ready = sem("p_turned"), sem("phi_done"), sem("p_ready")
        x_in = [sem(f"x_in{i}") for i in range(4)]
        x_turned, h_ready = sem("x_turned"), sem("h_ready")
        g_turned, g_ready = sem("g_turned"), sem("g_ready")
        lb_sem, lb_exp = sem("lb_step"), sem("lb_exp")
        pe_stored = [sem(f"pe_stored{i}") for i in range(4)]
        pe_in = [sem("pe_in0"), sem("pe_in1")]
        f_pre, f_exp, f_ln, f_cum, f_turned, cq_ready, c_stored = (
            sem(n) for n in ("f_pre", "f_exp", "f_ln", "f_cum", "f_turned", "cq_ready", "c_stored"))
        sq_ready, stats_done, rms_ready, qk_ready = sem("sq_ready"), sem("stats_done"), sem("rms_ready"), sem("qk_ready")
        vt_done, vtok_ready, tz_ready, zs_ready = sem("vt_done"), sem("vtok_ready"), sem("tz_ready"), sem("zs_ready")
        ck_in, ckm_ready = sem("ck_in"), sem("ckm_ready")
        scores_done, negm_ready, exp_ready = sem("scores_done"), sem("negm_ready"), sem("exp_ready")
        probs_ready, pt_done, pt_ready, pv_done = sem("probs_ready"), sem("pt_done"), sem("pt_ready"), sem("pv_done")
        hg_vt, hg_vtok, hg_tz = sem("hg_vt"), sem("hg_vtok"), sem("hg_tz")
        hg_qk, diag_done, level_ready, level_done, att_ready = (
            sem(n) for n in ("hg_qk", "diag_done", "level_ready", "level_done", "att_ready"))
        kst_done, kst_ready, u_done, state_ready = sem("kst_done"), sem("kst_ready"), sem("u_done"), sem("state_ready")
        ot_done, o_ready, osq_ready, ostat_done, orms_ready = (
            sem(n) for n in ("ot_done", "o_ready", "osq_ready", "ostat_done", "orms_ready"))
        thf_ready, tq_ready = sem("thf_ready"), sem("tq_ready")
        keys_ready, kmix_ready = sem("keys_ready"), sem("kmix_ready")
        outT_done, out_staged = sem("outT_done"), sem("out_staged")
        out_stored = [sem("out_stored0"), sem("out_stored1")]
        v_step = sem("v_step")

        def wait(eng, s, value):
            if not (isinstance(value, int) and value <= 0):
                eng.wait_ge(s, value)

        def end_of(k):
            return 2 * UPT - 1 if isinstance(k, int) and k == 0 else UPT * k + UPT

        def loop(eng, first, last, body):
            with eng.Fori(first, last) as i:
                body(i)

        block = ctx.enter_context(nc.Block())

        @block.sync
        def _(sp):
            def load(u, i, per, src, k=UB):
                n = u + per * i
                if not isinstance(n, int) or n >= RAW:
                    sp.wait_ge(lo_done, n - RAW + 1)
                dst = raw[:, u % RAW, :].rearrange("p (k n) -> p k n", k=k)
                sp.dma_start(dst, src).then_inc(w_loaded[u % RAW], 16)

            def tile_units(u, i, per, w, col):
                for j in range(UPT):
                    load(u + j, i, per, w[:, UB * j:UB * (j + 1), bass.ds(col, P)])

            for dst, src in ((ident[:, :], c_ident),
                             (grow[G_PRE:G_PRE + 2 * KT, :], pre_norm.rearrange("l (k p) -> (l k) p", p=P)),
                             (grow[G_POST:G_POST + 2 * KT, :], post_norm.rearrange("l (k p) -> (l k) p", p=P)),
                             (grow[G_LB:G_LB + 2 * KT, :], lb_logits.rearrange("l (k p) -> (l k) p", p=P)),
                             (grow[G_Q:G_Q + 1, :], g_q_fox), (grow[G_K:G_K + 1, :], g_k_fox),
                             (grow[G_O:G_O + 1, :], g_o_hg)):
                sp.dma_start(dst, src).then_inc(gvec_in, 16)
            for i in range(2):
                we = rows_of(w_pe[i])
                for j in range(PE_UNITS):
                    load(U_PE + j, i, PE_UNITS, we[:, :, 4 * P * j:4 * P * (j + 1)], k=PK)
            tile_units(U_F, 0, 0, wf, 4 * D + H - P)

            def fox_head(n):
                for j in range(4):
                    tile_units(U_FOX + UPT * j, n - 1, 4 * UPT, wf, n * P + (j * D - P))

            def hg_head(n):
                for j, part in enumerate((2, 1, 0, 3)):
                    tile_units(U_HG + UPT * j, n - 1, 4 * UPT, wh, n * P + (part * D - P))

            def square(u, w):
                def pair(i):
                    for j in range(2):
                        tile_units(u + UPT * j, i, 2 * UPT, w, (2 * i + j) * P)
                for m in range(2 * UPT):
                    half, j = m // 2, m % 2
                    load(u + m, 0, 0, w[:, UB * half:UB * (half + 1), j * P:(j + 1) * P])
                loop(sp, 2, KT // 2 + 1, lambda i: pair(i - 1))

            loop(sp, 1, H + 1, fox_head)
            square(U_OUT[0], wo[0])
            square(U_PG[0], wg[0])
            loop(sp, 1, H + 1, hg_head)
            square(U_OUT[1], wo[1])
            square(U_PG[1], wg[1])

        @block.gpsimd
        def _(pool):
            for i in range(2):
                pool.dma_start(pstage[i].rearrange("p (t n) -> p t n", t=TB),
                               p[i, 0].rearrange("(t p) n -> p t n", p=P)).then_inc(p_in[i], 16)

            def load_x(k, slot):
                if not (isinstance(k, int) and k < 4):
                    pool.wait_ge(x_turned, k - 3)
                pool.dma_start(xstage[slot].rearrange("p (t n) -> p t n", t=TB),
                               x_tok[:, :, bass.ds(k * P, P)]).then_inc(x_in[slot], 16)
            for k in range(4):
                load_x(k, k)
            for dst, src in ((causal[:, :], c_causal), (level_in, c_levels)):
                pool.dma_start(dst, src).then_inc(const_in, 16)
            pool.wait_ge(const_set, 1)
            pool.dma_start(bf_c[P - H:P, :], b_f_fox.rearrange("a h -> h a")).then_inc(bias_in, 16)

            def embed_unit(i, j, loads=True):
                if loads:
                    for m in range(2):
                        load_x(4 * i + 2 * j + m + 4, 2 * j + m)
                for f in range(4):
                    pool.wait_ge(tile_out, 8 * i + 4 * j + f + 1)
                    pool.dma_start(pe_scr[8 * i + 4 * j + f], pe_tile[f]).then_inc(pe_stored[f], 16)
            for i in range(PE_UNITS):
                for j in range(2):
                    embed_unit(i, j, loads=i < PE_UNITS - 1)

            pool.wait_ge(f_cum, 1)
            pool.dma_start(c_scr, fc[P - H:P, :]).then_inc(c_stored, 16)
            pool.wait_ge(c_stored, 16)

            def decay_row(g):
                if not isinstance(g, int):
                    pool.wait_ge(negm_ready, TB * g)
                pool.dma_start(ckb, c_scr[bass.ds(g, 1), :].to_broadcast([P, S])).then_inc(ck_in, 16)
                pool.wait_ge(ck_in, 16 * g + 16)
                pool.tensor_tensor(ckm.rearrange("p (t n) -> p t n", t=TB),
                                   ckb.rearrange("p (t n) -> p t n", t=TB),
                                   causal[:, :].unsqueeze(1).to_broadcast([P, TB, P]),
                                   ALU.subtract).then_inc(ckm_ready, 1)
            pool.wait_ge(const_in, 32)
            pool.wait_ge(f_ln, 2)
            pool.wait_ge(cq_ready, 1)
            decay_row(0)
            loop(pool, 1, H, decay_row)

            for lay in range(2):
                def split_y(k, lay=lay):
                    pool.wait_ge(xhi_done, KT * (3 * lay + 1) + k + 1)
                    pool.tensor_tensor(xlo[:, k], yT[:, k], xhi[:, k].bitcast(F32),
                                       ALU.subtract).then_inc(x_ready, 1)
                loop(pool, 0, KT - 1, split_y)

                def add_h(k, lay=lay):
                    pool.wait_ge(yn_ready, KT * lay + k + 1)
                    pool.tensor_tensor(hT[:, k], hT[:, k], yT[:, k], ALU.add).then_inc(hn_ready, 1)
                loop(pool, 0, KT, add_h)

                def load_pe(i, lay=lay):
                    for j in range(2):
                        if not isinstance(i, int):
                            pool.wait_ge(h_new, KT * lay + 2 * i + j - 1)
                        pool.dma_start(pe2[j], pe_scr[KT * lay + 2 * i + j]).then_inc(pe_in[j], 16)

                def store_out(i):
                    for j in range(2):
                        pool.wait_ge(out_staged, 2 * i + j + 1)
                        pool.dma_start(out_tok[:, :, bass.ds((2 * i + j) * P, P)],
                                       ostage2[j].rearrange("p (t n) -> p t n", t=TB)).then_inc(out_stored[j], 16)
                if lay == 0:
                    for j in range(4):
                        pool.wait_ge(pe_stored[j], 16 * (KT // 2))
                load_pe(0)
                if lay == 0:
                    loop(pool, 1, KT // 2, load_pe)
                else:
                    def turn(i):
                        load_pe(i)
                        store_out(i - 1)
                    loop(pool, 1, KT // 2, turn)
                    store_out(KT // 2 - 1)
            for j in range(2):
                pool.wait_ge(out_stored[j], 16 * KT // 2)

        @block.scalar
        def _(act):
            def split(u, i=0, per=0):
                n = u + per * i
                if isinstance(n, int) and n >= U_END:
                    return
                act.wait_ge(w_loaded[u % RAW], 16 * (u // RAW + 1) + (16 * per // RAW) * i)
                wait(act, w_used, n - RING + 1)
                act.activation(whi[:, u % RING].rearrange("p k n -> p (k n)"), raw[:, u % RAW, :],
                               ACT.Copy).then_inc(hi_done, 1)

            def split_h(lay, first, last, scaled=False):
                def one(k):
                    if not scaled:
                        act.wait_ge(hn_ready, KT * lay + k + 1)
                    scale = gcol[:, bass.ds(G_PRE + KT + k, 1)] if scaled else 1.0
                    act.activation(xhi[:, k], hT[:, k], ACT.Copy, scale=scale).then_inc(xhi_done, 1)
                if last - first == 1:
                    one(first)
                else:
                    loop(act, first, last, one)

            def split_y(lay, k):
                act.wait_ge(y_ready, KT * lay + k + 1)
                act.activation(xhi[:, k], yT[:, k], ACT.Copy).then_inc(xhi_done, 1)

            def token_rms(stage):
                act.wait_ge(norm_done, stage + 1)
                act.activation(rinv[:, :], bank[7][:, :], ACT.Sqrt, bias=eps_c, scale=1.0 / D).then_inc(norm_rms, 1)

            act.wait_ge(g_turned, 1)
            act.activation(gcol[:, 0:G_ROWS], bank[7][:, 0:G_ROWS], ACT.Copy).then_inc(g_ready, 1)
            for n in range(2 * PK):
                act.wait_ge(pt_p, n + 1)
                act.activation(xhi[:, KT - 2 * PK + n], bank[2 + n][:, :], ACT.Copy).then_inc(phi_done, 1)
            for u in range(HI_AHEAD):
                split(u)
            act.wait_ge(p_ready, 2 * PK)

            def take_x(k, slot):
                act.wait_ge(x_turned, k + 1)
                act.activation(hT[:, k], bank[2 + slot][:, :], ACT.Copy).then_inc(h_ready, 1)
                wait(act, acc_step, k - 1)
                act.activation(sq2[slot], bank[2 + slot][:, :], ACT.Square).then_inc(sq_done, 1)

            def split_x(k):
                act.wait_ge(h_ready, k + 1)
                act.activation(xhi[:, k], hT[:, k], ACT.Copy,
                               scale=gcol[:, G_PRE + k:G_PRE + k + 1]).then_inc(xhi_done, 1)
            act.wait_ge(lb_sem, 2)
            act.activation(lbc[:, 0:2], lbc[:, 0:2], ACT.Exp).then_inc(lb_exp, 1)
            for u in range(2 * PE_UNITS):
                split(U_PE + u + HI_AHEAD)
                for slot in range(2):
                    take_x(2 * u + slot, slot)
                split_x(u)
            for k in range(2 * PE_UNITS, KT):
                if k == KT - 2 * PK:
                    act.wait_ge(w_used, U_F)
                split_x(k)
            split(U_F + HI_AHEAD)
            token_rms(0)
            split(U_F + 1 + HI_AHEAD)
            act.wait_ge(f_pre, 1)
            act.activation(fa[FR, :], fl[FR, :], ACT.Abs).then_inc(f_exp, 1)
            act.wait_ge(f_exp, 1)
            act.activation(fa[FR, :], fa[FR, :], ACT.Exp, scale=-1.0).then_inc(f_exp, 1)
            act.wait_ge(f_exp, 2)
            act.activation(fa[FR, :], fa[FR, :], ACT.Ln, bias=one_c[FR, :]).then_inc(f_ln, 1)

            def fox_head(h, proj=True, attn=True, first=False, fill=None):
                g = h - 1
                for u in range(4 * UPT):
                    if proj:
                        split(U_FOX + u + HI_AHEAD, h, 4 * UPT)
                    elif fill is not None:
                        fill(u)
                    if first and u == 4:
                        act.wait_ge(f_turned, 1)
                        act.activation(cq[:, :, :], bank[6][:, 0:TB * 32].rearrange("p (t n) -> p t n", t=TB),
                                       ACT.Copy).then_inc(cq_ready, 1)
                        for n in range(4):
                            act.wait_ge(pe_stored[n], 16 * (KT // 2))
                    if attn and u == 0:
                        act.wait_ge(stats_done, 2 * g + 1)
                        act.activation(sqq, bank[2][:, :], ACT.Sqrt, bias=eps_c, scale=1.0 / P).then_inc(rms_ready, 1)
                        act.wait_ge(stats_done, 2 * g + 2)
                        act.activation(sqk, bank[3][:, :], ACT.Sqrt, bias=eps_c, scale=1.0 / P).then_inc(rms_ready, 1)
                    if attn and u == 2:
                        act.wait_ge(vt_done, g + 1)
                        act.activation(vtok, bank[4][:, :], ACT.Copy).then_inc(vtok_ready, 1)
                        act.wait_ge(tile_out, T_FOX + 4 * g + 4)
                        act.activation(tz_t, z_t, ACT.Tanh).then_inc(tz_ready, 1)
                    if attn and u == 4:
                        for t in range(TB):
                            pr = prob[:, prob_at[t]:prob_at[t] + (t + 1) * P]
                            act.wait_ge(negm_ready, TB * g + t + 1)
                            act.activation(pr, pr, ACT.Exp, bias=negm[:, t:t + 1],
                                           accum_out=rsum[:, t:t + 1]).then_inc(exp_ready, 1)
                    if attn and u == 6:
                        act.wait_ge(pt_done, g + 1)
                        act.activation(probT[:, 0:512], bank[2][:, :], ACT.Copy)
                        act.activation(probT[:, 512:896], bank[3][:, 0:384], ACT.Copy)
                        act.activation(probT[:, 1152:1280], bank[3][:, 384:512], ACT.Copy)
                        act.activation(probT[:, 896:1152], bank[4][:, 0:256], ACT.Copy).then_inc(pt_ready, 1)
                    if proj and u == 4:
                        act.wait_ge(tile_out, T_FOX + 4 * h + 1)
                        act.activation(sqq, q_t, ACT.Square).then_inc(sq_ready, 1)
                    if proj and u == 5:
                        act.wait_ge(tile_out, T_FOX + 4 * h + 2)
                        act.activation(sqk, k_t, ACT.Square).then_inc(sq_ready, 1)

            def mix_keys(lv, g):
                n = 1 << lv
                act.wait_ge(keys_ready, (LEVELS + 1) * g + lv + 1)
                for pair in range(TB // 2):
                    keys = bass.AP(k_t.tensor, k_t.offset + 2 * P * pair,
                                   [list(k_t.ap[0]), [2 * n, P // (2 * n)], [P + n, 2], [1, n]])
                    ins = act.activation(kmix[:, pair].rearrange("p (b e n) -> p b e n", e=2, n=n), keys, ACT.Copy)
                ins.then_inc(kmix_ready, 1)

            def hg_head(h, proj=True, attn=True, first=False, fill=None):
                g = h - 1
                for u in range(4 * UPT):
                    if proj:
                        split(U_HG + u + HI_AHEAD, h, 4 * UPT)
                    elif fill is not None:
                        fill(u)
                    if first and u == 2:
                        token_rms(2)
                    if attn and u == 0:
                        act.wait_ge(hg_vt, g + 1)
                        act.activation(vtok, bank[4][:, :], ACT.Copy).then_inc(hg_vtok, 1)
                    if attn and 1 <= u < 4:
                        mix_keys(2 * u, g)
                    if attn and u < 3:
                        mix_keys(2 * u + 1, g)
                    if attn and u == 2:
                        act.wait_ge(tile_out, N_HG + 4 * g + 4)
                        act.activation(tz_t, z_t, ACT.Tanh).then_inc(hg_tz, 1)
                    if attn and u == 4:
                        act.wait_ge(kst_done, g + 1)
                        act.activation(kst[:, 0:3 * P], bank[4][:, 0:3 * P], ACT.Copy).then_inc(kst_ready, 1)
                    if proj and u == 5:
                        act.wait_ge(tile_out, N_HG + 4 * h + 2)
                        act.activation(f_t, f_t, ACT.Tanh, scale=0.5).then_inc(thf_ready, 1)
                    if attn and u == 5:
                        act.wait_ge(o_ready, g + 1)
                        act.activation(osq, o_t, ACT.Square).then_inc(osq_ready, 1)
                    if attn and u == 6:
                        act.wait_ge(ostat_done, g + 1)
                        act.activation(osq, bank[7][:, :], ACT.Sqrt, bias=eps_c, scale=1.0 / P).then_inc(orms_ready, 1)
                    if proj and u == 6:
                        mix_keys(0, h)
                    if proj and u == 7:
                        act.wait_ge(tile_out, N_HG + 4 * h + 3)
                        act.activation(tq_t, q_t, ACT.Tanh).then_inc(tq_ready, 1)

            for lay, head in enumerate((fox_head, hg_head)):
                head(0, attn=False, first=True)
                loop(act, 1, H, head)
                def fill(u, lay=lay):
                    first, last, units = (FOX_HI, HG_HI)[lay].get(u, (0, 0, []))
                    for k in range(first, last):
                        split_y(lay, k)
                    for m in units:
                        split(U_OUT[lay] + m)
                act.wait_ge(w_used, U_OUT[lay])
                head(H, proj=False, fill=fill)
                split_y(lay, KT - 1)
                split(U_OUT[lay] + 2 * UPT + 2)

                def out_pair(i, lay=lay):
                    for j in range(2):
                        if not (isinstance(i, int) and i == 0):
                            for m in range(UPT):
                                split(U_OUT[lay] + UPT * j + m + HI_AHEAD, i, 2 * UPT)
                        k = 2 * i + j
                        act.wait_ge(yo_ready, KT * lay + k + 1)
                        if not (isinstance(i, int) and i == 0):
                            act.wait_ge(acc_step, (KT - 1) * (2 * lay + 1) + k - 1)
                        act.activation(sq2[j], yT[:, k], ACT.Square).then_inc(sq_done, 1)
                out_pair(0)
                loop(act, 1, KT // 2, out_pair)
                split(U_PG[lay] + HI_AHEAD)
                token_rms(2 * lay + 1)
                split_h(lay, 0, KT - 2)
                for m in (1, 2):
                    split(U_PG[lay] + HI_AHEAD + m)
                    split_h(lay, KT - 3 + m, KT - 2 + m)
                split(U_PG[lay] + HI_AHEAD + 3)

                def gate_pair(i, lay=lay, last=False):
                    for j in range(2):
                        k = 2 * i + j
                        if not (isinstance(i, int) and i == 0):
                            for m in range(UPT):
                                split(U_PG[lay] + UPT * j + m + HI_AHEAD, i, 2 * UPT)
                        act.wait_ge(w_used, U_PG[lay] + end_of(k))
                        if not (isinstance(i, int) and i == 0):
                            act.wait_ge(h_new, KT * lay + k - 1)
                        src = bank[GATE_BANKS[j] if isinstance(i, int) and i == 0 else T_PG[lay] % 2 ^ j]
                        act.activation(tg2[j], src[:, :], ACT.Tanh, scale=0.5).then_inc(tg_ready, 1)
                        if last and j == 1:
                            split_h(lay, 0, 3, scaled=True)
                        if lay == 0:
                            act.wait_ge(h_new, k + 1)
                            if not (isinstance(i, int) and i == 0):
                                act.wait_ge(acc_step, 2 * (KT - 1) + k - 1)
                            act.activation(sq2[j], hT[:, k], ACT.Square).then_inc(sq_done, 1)
                        elif not (isinstance(k, int) and k == 0):
                            stage_out(k - 1, 1 - j)

                def stage_out(k, slot):
                    act.wait_ge(outT_done, k + 1)
                    if not isinstance(k, int):
                        if slot == 0:
                            act.wait_ge(out_stored[0], 8 * k)
                        else:
                            act.wait_ge(out_stored[1], 8 * k - 8)
                    elif k >= 2:
                        act.wait_ge(out_stored[slot], 16 * (k // 2))
                    act.activation(ostage2[slot], bank[2 + slot][:, :], ACT.Copy).then_inc(out_staged, 1)

                gate_pair(0)
                if lay == 0:
                    loop(act, 1, KT // 2 - 1, gate_pair)
                    gate_pair(KT // 2 - 1, last=True)
                    split_h(lay, 3, KT, scaled=True)
                else:
                    gate_pair(1)
                    loop(act, 2, KT // 2 - 1, gate_pair)
                    gate_pair(KT // 2 - 1)
                    stage_out(KT - 1, 1)

        @block.vector
        def _(dve):
            steps = {"fixed": 0, "turn": None}

            def link(ins):
                ins.then_inc(v_step, 1)
                steps["fixed"] += 1
                turn = steps["turn"]
                dve.wait_ge(v_step, steps["fixed"] if turn is None else steps["fixed"] + turn)

            def linked_loop(first, last, links, body):
                start = steps["fixed"]
                with dve.Fori(first, last) as i:
                    steps["turn"] = links * (i - first)
                    body(i)
                    steps["turn"] = None
                assert steps["fixed"] == start + links, steps["fixed"] - start
                steps["fixed"] = start + links * (last - first)

            def split(u, i=0, per=0):
                n = u + per * i
                if isinstance(n, int) and n >= U_END:
                    return
                dve.wait_ge(hi_done, n + 1)
                wait(dve, w_used, n - RING + 1)
                dve.tensor_tensor(wlo[:, u % RING].rearrange("p k n -> p (k n)"), raw[:, u % RAW, :],
                                  whi[:, u % RING].rearrange("p k n -> p (k n)").bitcast(F32),
                                  ALU.subtract).then_inc(lo_done, 1)

            def split_one(stage, src, k):
                dve.wait_ge(xhi_done, KT * stage + k + 1)
                dve.tensor_tensor(xlo[:, k], src[:, k], xhi[:, k].bitcast(F32), ALU.subtract).then_inc(x_ready, 1)

            def split_scaled(stage, scale_at, first, last):
                def one(k):
                    dve.wait_ge(xhi_done, KT * stage + k + 1)
                    dve.scalar_tensor_tensor(xlo[:, k], hT[:, k], gcol[:, bass.ds(scale_at + k, 1)],
                                             xhi[:, k].bitcast(F32), ALU.mult, ALU.subtract).then_inc(x_ready, 1)
                loop(dve, first, last, one)

            def zero_acc():
                link(dve.memset(acc, 0.0))

            def add_square(k, stage, slot):
                if isinstance(k, int) and k == KT - 1:
                    return
                dve.wait_ge(sq_done, KT * stage + k + 1)
                wait(dve, acc_step, (KT - 1) * stage + k)
                dve.tensor_tensor(acc, acc, sq2[slot], ALU.add).then_inc(acc_step, 1)

            def token_rinv(stage):
                dve.wait_ge(norm_rms, stage + 1)
                dve.reciprocal(rinv[:, :], rinv[:, :]).then_inc(norm_ready, 1)
                dve.wait_ge(norm_ready, stage + 1)

            def take_tile(t0, used, dst, halve=False):
                dve.wait_ge(w_used, used)
                src = bank[t0 % 2][:, :]
                if halve:
                    dve.scalar_tensor_tensor(dst, src, 0.5, rinv[:, :], ALU.mult, ALU.mult).then_inc(tile_out, 1)
                else:
                    dve.tensor_tensor(dst, src, rinv[:, :], ALU.mult).then_inc(tile_out, 1)

            def reversed_chunks(tile):
                return chunks(tile, 1)[:, :, ::-1]

            def chunks(tile, x):
                return tile.rearrange("p (a x n) -> p a x n", x=2, n=P)[:, :, x]

            def take_hg_tile(t0, used, dst, halve=False):
                dve.wait_ge(w_used, used)
                for x in range(2):
                    to = reversed_chunks(dst) if x else chunks(dst, x)
                    src, r = chunks(bank[t0 % 2][:, :], x), chunks(rinv[:, :], x)
                    if halve:
                        ins = dve.scalar_tensor_tensor(to, src, 0.5, r, ALU.mult, ALU.mult)
                    else:
                        ins = dve.tensor_tensor(to, src, r, ALU.mult)
                ins.then_inc(tile_out, 1)

            dve.memset(small[:, 2:3], 0.0)
            dve.memset(ones[:, :], 1.0).then_inc(const_set, 1)
            dve.memset(eps_c, EPS)
            dve.memset(one_c, 1.0)
            dve.memset(acc, 0.0)
            link(dve.memset(small[:, 3:4], 0.0))
            for n in range(2 * PK):
                dve.wait_ge(phi_done, n + 1)
                dve.tensor_tensor(xlo[:, KT - 2 * PK + n], bank[2 + n][:, :],
                                  xhi[:, KT - 2 * PK + n].bitcast(F32), ALU.subtract).then_inc(p_ready, 1)
            for u in range(LO_AHEAD):
                split(u)
            dve.wait_ge(g_ready, 1)
            link(dve.tensor_scalar(gcol[:, G_Q:G_Q + 1], gcol[:, G_Q:G_Q + 1], float(P) ** -0.5, None, ALU.mult))
            l0, l1 = gcol[:, G_LB:G_LB + KT], gcol[:, G_LB + KT:G_LB + 2 * KT]
            link(dve.tensor_tensor(lbc[:, 2], l0, l1, ALU.max))
            dve.tensor_tensor(lbc[:, 0], l0, lbc[:, 2], ALU.subtract).then_inc(lb_sem, 1)
            dve.tensor_tensor(lbc[:, 1], l1, lbc[:, 2], ALU.subtract).then_inc(lb_sem, 1)

            dve.wait_ge(lb_exp, 1)
            link(dve.tensor_tensor(lbc[:, 2], lbc[:, 0], lbc[:, 1], ALU.add))
            link(dve.reciprocal(lbc[:, 2], lbc[:, 2]))
            dve.tensor_tensor(lbc[:, 3], lbc[:, 0], lbc[:, 2], ALU.mult)
            link(dve.tensor_tensor(lbc[:, 5], lbc[:, 1], lbc[:, 2], ALU.mult))
            link(dve.tensor_tensor(lbc[:, 4], lbc[:, 3], lbc[:, 5], ALU.add))
            link(dve.tensor_tensor(lbc[:, 4], lbc[:, 4], lbc[:, 3], ALU.subtract))
            link(dve.tensor_scalar(lbc[:, 5], lbc[:, 4], -1.0, 1.0, ALU.mult, ALU.add))
            lower, upper = lbc[:, 4], lbc[:, 5]

            def split_h(k):
                dve.wait_ge(xhi_done, k + 1)
                dve.scalar_tensor_tensor(xlo[:, k], hT[:, k], gcol[:, G_PRE + k:G_PRE + k + 1],
                                         xhi[:, k].bitcast(F32), ALU.mult, ALU.subtract).then_inc(x_ready, 1)
            for u in range(2 * PE_UNITS):
                split(U_PE + u + LO_AHEAD)
                for f in range(4):
                    if f < 3:
                        dve.wait_ge(embed_done, 3 * u + f + 1)
                    else:
                        dve.wait_ge(w_used, u + 1)
                    wait(dve, pe_stored[f], 16 * u)
                    dve.tensor_copy(pe_tile[f], bank[embed_banks[f]][:, :]).then_inc(tile_out, 1)
                    if f == 1 and u:
                        add_square(2 * u - 1, 0, 1)
                    if f == 3:
                        add_square(2 * u, 0, 0)
                split_h(u)
            for k in range(2 * PE_UNITS, KT):
                split_h(k)
            split(U_F + LO_AHEAD)
            token_rinv(0)
            split(U_F + 1 + LO_AHEAD)
            dve.wait_ge(const_in, 32)
            for x in range(2):
                for pair in range(TB // 2):
                    at = (x * TB // 2 + pair) * P // 2
                    ins = dve.tensor_copy(levels[:, :, at:at + P // 2],
                                          level_in.rearrange("p (l x n) -> p l x n", l=LEVELS, x=2)[:, :, x])
            link(ins)
            dve.wait_ge(pe_stored[3], 16 * 2 * PE_UNITS)
            link(dve.memset(fone, 1.0))
            dve.wait_ge(w_used, U_F + UPT)
            dve.tensor_tensor(fl[FR, :], bank[T_F % 2][FR, :], rinv[FR, :], ALU.mult).then_inc(tile_out, 1)
            dve.wait_ge(tile_out, T_F + 1)
            dve.wait_ge(bias_in, 16)
            dve.tensor_scalar(fl[FR, :], fl[FR, :], bf_c[FR, :], None, ALU.add).then_inc(f_pre, 1)
            dve.wait_ge(f_ln, 1)
            dve.scalar_tensor_tensor(fl[FR, :], fl[FR, :], 0.0, fa[FR, :], ALU.min, ALU.subtract).then_inc(f_ln, 1)
            dve.wait_ge(f_ln, 2)
            dve.tensor_tensor_scan(fc[FR, :], fone[FR, :], fl[FR, :], 0.0, ALU.mult, ALU.add).then_inc(f_cum, 1)

            def fox_head(h, proj=True, attn=True, fill=None):
                g = h - 1
                for u in range(4 * UPT):
                    if proj:
                        split(U_FOX + u + LO_AHEAD, h, 4 * UPT)
                    elif fill is not None:
                        fill(u)
                    if attn and u == 0:
                        take_tile(T_FOX + 3, U_FOX + 4 * UPT * g + 4 * UPT, z_t, halve=True)
                    if attn and u in (0, 1):
                        r, t, gc = ((sqq, q_t, G_Q), (sqk, k_t, G_K))[u]
                        dve.wait_ge(rms_ready, 2 * g + u + 1)
                        link(dve.reciprocal(r, r))
                        dve.scalar_tensor_tensor(t, t, gcol[:, gc:gc + 1], r, ALU.mult, ALU.mult).then_inc(qk_ready, 1)
                    if attn and u == 2:
                        dve.wait_ge(tz_ready, g + 1)
                        dve.scalar_tensor_tensor(tz_t, tz_t, 1.0, z_t, ALU.add, ALU.mult).then_inc(zs_ready, 1)
                    if attn and u == 3:
                        dve.wait_ge(scores_done, g + 1)
                    if proj and u == 3:
                        take_tile(T_FOX, U_FOX + 4 * UPT * h + 1 * UPT, q_t)
                    if attn and u == 3:
                        dve.wait_ge(ckm_ready, g + 1)
                        for t in range(TB):
                            at, n = prob_at[t], t * P
                            src = score_of(t)
                            c_query = cq[:, t, bass.ds(32 - H + g, 1)]
                            if t:
                                dve.scalar_tensor_tensor(prob[:, at:at + n], src[:, 0:n], c_query, ckb[:, 0:n],
                                                         ALU.add, ALU.subtract)
                            ins = dve.scalar_tensor_tensor(prob[:, at + n:at + n + P], src[:, n:n + P], c_query,
                                                           ckm[:, n:n + P], ALU.add, ALU.subtract)
                        link(ins)
                        for t in range(TB):
                            dve.tensor_reduce(negm[:, t:t + 1], prob[:, prob_at[t]:prob_at[t] + (t + 1) * P],
                                              AX.X, ALU.max, negate=True).then_inc(negm_ready, 1)
                    if proj and u == 4:
                        take_tile(T_FOX + 1, U_FOX + 4 * UPT * h + 2 * UPT, k_t)
                    if attn and u == 5:
                        dve.wait_ge(exp_ready, TB * g + TB)
                        link(dve.reciprocal(rsum, rsum))
                        for t in range(TB):
                            pr = prob[:, prob_at[t]:prob_at[t] + (t + 1) * P]
                            ins = dve.tensor_scalar(pr, pr, rsum[:, t:t + 1], None, ALU.mult)
                        ins.then_inc(probs_ready, 1)
                    if proj and u == 6:
                        take_tile(T_FOX + 2, U_FOX + 4 * UPT * h + 3 * UPT, v_t)
                    if attn and u == 7:
                        dve.wait_ge(pv_done, g + 1)
                        dve.wait_ge(zs_ready, g + 1)
                        dve.tensor_tensor(yT[:, g], bank[5][:, :], tz_t, ALU.mult).then_inc(y_ready, 1)

            def score_of(t):
                return {0: bank[6][:, 384:512], 1: bank[7][:, 0:256], 2: bank[6][:, 0:384], 3: bank[5][:, :]}[t]

            def tree_of(lv):
                if lv == 0:
                    return f_t
                at = S - (S >> (lv - 1))
                return tree[:, at:at + (S >> lv)]

            def hg_head(h, proj=True, attn=True, first=False, fill=None):
                g = h - 1

                def level(lv):
                    n = 1 << lv
                    dve.wait_ge(level_done, LEVELS * g + lv + 1)
                    dve.wait_ge(level_ready, (LEVELS + 1) * g + lv + 1)
                    if lv:
                        dve.wait_ge(att_ready, LEVELS * g + lv)
                    nb = P // (2 * n)
                    t = tree_of(lv).rearrange("p (a x b e) -> p a x b e", x=2, b=nb, e=2)
                    q, k, pairs = (tile.rearrange("p (a x b e n) -> p a x b e n", x=2, b=nb, e=2, n=n)
                                   for tile in (q_t, k_t, att))
                    for x in range(2):
                        ins = dve.tensor_tensor(k[:, :, x, :, x], k[:, :, x, :, x],
                                                t[:, :, x, :, 1 - x:2 - x].to_broadcast([P, TB // 2, nb, n]), ALU.mult)
                    ins.then_inc(keys_ready, 1)
                    for x in range(2):
                        dve.tensor_tensor(q[:, :, x, :, 1 - x], q[:, :, x, :, 1 - x],
                                          t[:, :, x, :, x:x + 1].to_broadcast([P, TB // 2, nb, n]), ALU.mult)
                    both = tree_of(lv).rearrange("p (b e) -> p b e", e=2)
                    dve.tensor_tensor(tree_of(lv + 1), both[:, :, 0], both[:, :, 1], ALU.mult).then_inc(level_ready, 1)
                    for x in range(2):
                        mask = levels[:, lv].rearrange("p (x a b n) -> p x a b n", x=2, a=TB // 2, n=n)[:, x]
                        src = bank[2 + lv % 2][:, 0:S // 2].rearrange("p (a x b n) -> p a x b n", x=2, b=nb, n=n)
                        ins = dve.copy_predicated(pairs[:, :, x, :, 1 - x], mask, src[:, :, x])
                    ins.then_inc(att_ready, 1)

                for u in range(4 * UPT):
                    if attn and u == 0:
                        dve.wait_ge(diag_done, g + 1)
                        dve.tensor_tensor(att.rearrange("p (t n) -> p t n", t=TB),
                                          bank[5][:, :].rearrange("p (t n) -> p t n", t=TB),
                                          ident[:, :].unsqueeze(1).to_broadcast([P, TB, P]), ALU.mult)
                        dve.tensor_tensor(q_t, q_t, f_t, ALU.mult).then_inc(level_ready, 1)
                    if attn and 1 <= u < 4:
                        level(2 * u - 1)
                    if proj:
                        split(U_HG + u + LO_AHEAD, h, 4 * UPT)
                    elif fill is not None:
                        fill(u)
                    if attn and u < 4:
                        level(2 * u)
                    if attn and u == 0:
                        take_tile(T_HG + 3, U_HG + 4 * UPT * g + 4 * UPT, z_t, halve=True)
                    if first and u == 2:
                        token_rinv(2)
                    if proj and u == 2:
                        if attn:
                            dve.wait_ge(hg_vt, g + 1)
                        take_hg_tile(T_HG, U_HG + 4 * UPT * h + 1 * UPT, v_t)
                    if proj and u == 4:
                        take_hg_tile(T_HG + 1, U_HG + 4 * UPT * h + 2 * UPT, f_t)
                    if attn and u == 4:
                        dve.wait_ge(u_done, g + 1)
                        dve.wait_ge(level_ready, (LEVELS + 1) * (g + 1))
                        total = tree_of(LEVELS)
                        link(dve.tensor_copy(st[:, 0:P], bank[5][:, 0:P]))
                        link(dve.scalar_tensor_tensor(st[:, P:2 * P], st[:, 0:P], total[:, 1:2],
                                                      bank[5][:, P:2 * P], ALU.mult, ALU.add))
                        dve.scalar_tensor_tensor(st[:, 2 * P:3 * P], st[:, P:2 * P], total[:, 2:3],
                                                 bank[5][:, 2 * P:3 * P], ALU.mult, ALU.add).then_inc(state_ready, 1)
                    if attn and u == 5:
                        dve.wait_ge(ot_done, g + 1)
                        dve.tensor_copy(chunks(o_t, 0), chunks(bank[6][:, :], 0))
                        dve.tensor_copy(reversed_chunks(o_t), chunks(bank[6][:, :], 1)).then_inc(o_ready, 1)
                    if proj and u == 5:
                        dve.wait_ge(thf_ready, h + 1)
                        link(dve.tensor_scalar(f_t, f_t, 0.5, 0.5, ALU.mult, ALU.add))
                        link(dve.tensor_scalar(f_t, f_t, upper[:, bass.ds(h, 1)], lower[:, bass.ds(h, 1)],
                                               ALU.mult, ALU.add))
                        dve.tensor_scalar(k_t, f_t, -1.0, 1.0, ALU.mult, ALU.add).then_inc(keys_ready, 1)
                    if proj and u == 6:
                        take_hg_tile(T_HG + 2, U_HG + 4 * UPT * h + 3 * UPT, q_t, halve=True)
                    if attn and u == 6:
                        dve.wait_ge(orms_ready, g + 1)
                        link(dve.reciprocal(osq, osq))
                        dve.wait_ge(o_ready, g + 1)
                        dve.scalar_tensor_tensor(o_t, o_t, gcol[:, G_O:G_O + 1], osq, ALU.mult, ALU.mult)
                    if proj and u == 7:
                        dve.wait_ge(tq_ready, h + 1)
                        dve.wait_ge(tile_out, N_HG + 4 * h + 3)
                        dve.scalar_tensor_tensor(q_t, tq_t, 1.0, q_t, ALU.add, ALU.mult).then_inc(hg_qk, 1)
                    if attn and u == 7:
                        dve.wait_ge(hg_tz, g + 1)
                        link(dve.scalar_tensor_tensor(tz_t, tz_t, 1.0, z_t, ALU.add, ALU.mult))
                        dve.tensor_tensor(yT[:, g], o_t, tz_t, ALU.mult).then_inc(y_ready, 1)

            for lay, (head, links) in enumerate(((fox_head, 4), (hg_head, 6))):
                if lay:
                    head(0, attn=False, first=True)
                else:
                    head(0, attn=False)
                linked_loop(1, H, links, head)

                def fill(u, lay=lay):
                    for m in (FOX_LO, HG_LO)[lay].get(u, []):
                        split(U_OUT[lay] + m)
                head(H, proj=False, fill=fill)
                dve.wait_ge(x_ready, KT * (3 * lay + 1) + KT - 1)
                split_one(3 * lay + 1, yT, KT - 1)
                zero_acc()

                def out_pair(i, lay=lay):
                    for j in range(2):
                        k = 2 * i + j
                        if not (isinstance(i, int) and i == 0):
                            for m in range(UPT):
                                split(U_OUT[lay] + UPT * j + m + LO_AHEAD, i, 2 * UPT)
                        dve.wait_ge(w_used, U_OUT[lay] + end_of(k))
                        dve.tensor_copy(yT[:, k], bank[T_OUT[lay] % 2 ^ j][:, :]).then_inc(yo_ready, 1)
                        add_square(k, 2 * lay + 1, j)
                out_pair(0)
                loop(dve, 1, KT // 2 - 1, out_pair)
                out_pair(KT // 2 - 1)
                for m in range(LO_AHEAD, 2 * UPT):
                    split(U_PG[lay] + m)
                token_rinv(2 * lay + 1)

                def scale_y(k, lay=lay):
                    dve.scalar_tensor_tensor(yT[:, k], yT[:, k], gcol[:, bass.ds(G_POST + KT * lay + k, 1)],
                                             rinv[:, :], ALU.mult, ALU.mult).then_inc(yn_ready, 1)

                def scale_and_split(k, lay=lay):
                    scale_y(k)
                    split_one(3 * lay + 2, hT, k - NORM_LAG)
                for k in range(NORM_LAG):
                    scale_y(k)
                loop(dve, NORM_LAG, KT, scale_and_split)
                for k in range(KT - NORM_LAG, KT):
                    split_one(3 * lay + 2, hT, k)
                    if k >= KT - 2:
                        split(U_PG[lay] + 2 * UPT + k - KT + 2)
                if lay == 0:
                    zero_acc()

                def gate_pair(i, lay=lay, last=False):
                    for j in range(2):
                        k = 2 * i + j
                        if not (isinstance(i, int) and i == 0):
                            for m in range(UPT):
                                split(U_PG[lay] + UPT * j + m + LO_AHEAD, i, 2 * UPT)
                        dve.wait_ge(tg_ready, KT * lay + k + 1)
                        dve.wait_ge(pe_in[j], 16 * (KT // 2) * lay + 16 * i + 16)
                        link(dve.scalar_tensor_tensor(tg2[j], tg2[j], 1.0, pe2[j], ALU.add, ALU.mult))
                        if lay and not isinstance(i, int):
                            dve.wait_ge(outT_done, k - 1)
                        dst = hout2[j] if lay else hT[:, k]
                        dve.scalar_tensor_tensor(dst, tg2[j], 0.5, hT[:, k], ALU.mult, ALU.add).then_inc(h_new, 1)
                        if last and j == 1:
                            split_scaled(3, G_PRE + KT, 0, 3)
                        if lay == 0:
                            add_square(k, 2, j)
                gate_pair(0)
                if lay == 0:
                    linked_loop(1, KT // 2 - 1, 2, gate_pair)
                    gate_pair(KT // 2 - 1, last=True)
                    split_scaled(3, G_PRE + KT, 3, KT)
                else:
                    linked_loop(1, KT // 2 - 1, 2, gate_pair)
                    dve.wait_ge(outT_done, KT - 2)
                    gate_pair(KT // 2 - 1)

        @block.tensor
        def _(pe):
            def product(dst, u, b, k, first, last):
                hi, lo = whi[:, u % RING, b], wlo[:, u % RING, b]
                pe.matmul(dst, hi, xhi[:, k], start=first, stop=False)
                pe.matmul(dst, hi, xlo[:, k], start=False, stop=False)
                return pe.matmul(dst, lo, xhi[:, k], start=False, stop=last)

            def unit(u, i, per, t0, t, half, freed=tile_out, stage=None, mid=None):
                pe.wait_ge(lo_done, u + per * i + 1)
                if half == 0:
                    wait(pe, freed, t - 1)
                for b in range(UB):
                    k = UB * half + b
                    if stage is not None:
                        pe.wait_ge(x_ready, KT * stage + k + 1)
                    ins = product(bank[t0 % 2][:, :], u, b, k, k == 0, k == KT - 1)
                    if b == UB // 2 - 1 and mid is not None:
                        mid()
                ins.then_inc(w_used, 1)

            def piece(u0, banks, stage, m, first, last):
                half, j = m // 2, m % 2
                if first == 0:
                    pe.wait_ge(lo_done, u0 + m + 1)
                for b in range(first, last):
                    k = UB * half + b
                    pe.wait_ge(x_ready, KT * stage + k + 1)
                    ins = product(bank[banks[j]][:, :], u0 + m, b, k, k == 0, k == KT - 1)
                    if b == UB - 1:
                        ins.then_inc(w_used, 1)

            def turn(dst, src, n, ins=None):
                for t in range(n):
                    ins = pe.transpose(dst[:, t * P:(t + 1) * P], src[:, t * P:(t + 1) * P], ident[:, :])
                return ins

            def sum_squares(stage):
                pe.wait_ge(acc_step, (KT - 1) * (stage + 1))
                pe.matmul(bank[7][:, :], ones[:, :], acc, start=True, stop=False)
                pe.wait_ge(sq_done, KT * (stage + 1))
                pe.matmul(bank[7][:, :], ones[:, :], sq2[1], start=False, stop=True).then_inc(norm_done, 1)

            pe.wait_ge(gvec_in, 112)
            pe.transpose(bank[7][:, 0:G_ROWS], grow[0:G_ROWS, :], ident[0:G_ROWS, 0:G_ROWS]).then_inc(g_turned, 1)
            for i in range(2):
                pe.wait_ge(p_in[i], 16)
                for k in range(PK):
                    for t in range(TB):
                        at = t * PLE + k * P
                        ins = pe.transpose(bank[2 + PK * i + k][:, t * P:(t + 1) * P],
                                           pstage[i][:, at:at + P], ident[:, :])
                    ins.then_inc(pt_p, 1)
            pe.wait_ge(p_ready, 2 * PK)

            def turn_x(k):
                pe.wait_ge(x_in[k % 4], 16 * (k // 4) + 16)
                wait(pe, sq_done, k - 1)
                turn(bank[2 + k % 2], xstage[k % 4], TB).then_inc(x_turned, 1)
            for u in range(2 * PE_UNITS):
                i, j = u // PE_UNITS, u % PE_UNITS
                pe.wait_ge(lo_done, u + 1)
                for f in range(4):
                    wait(pe, tile_out, 4 * u + f - 3)
                    for k in range(PK):
                        at = KT - 2 * PK + PK * i + k
                        ins = product(bank[embed_banks[f]][:, :], u, 4 * k + f, at, k == 0, k == PK - 1)
                    ins.then_inc(embed_done if f < 3 else w_used, 1)
                    if f % 2:
                        turn_x(2 * u + f // 2)
            unit(U_F, 0, 0, T_F, T_F, 0, stage=0)
            sum_squares(0)
            unit(U_F + 1, 0, 0, T_F, T_F, 1, stage=0)
            def turn_c():
                pe.wait_ge(f_cum, 1)
                for t in range(TB):
                    ins = pe.transpose(bank[6][:, 32 * t:32 * (t + 1)], fc[FR, t * P:(t + 1) * P], ident[FR, FR])
                ins.then_inc(f_turned, 1)

            def fox_head(h, proj=True, attn=True, first=False, fill=None):
                g = h - 1
                for u in range(4 * UPT):
                    if attn and u == 0:
                        pe.wait_ge(tile_out, T_FOX + 4 * g + 3)
                        turn(bank[4], v_t, TB).then_inc(vt_done, 1)
                        for n, sq in enumerate((sqq, sqk)):
                            pe.wait_ge(sq_ready, 2 * g + n + 1)
                            pe.matmul(bank[2 + n][:, :], ones[:, :], sq, start=True, stop=True).then_inc(stats_done, 1)
                    if proj:
                        j = u // UPT
                        unit(U_FOX + u, h, 4 * UPT, T_FOX + j, T_FOX + 4 * h + j, u % UPT)
                    elif fill is not None:
                        fill(u)
                    if first and u == 3:
                        turn_c()
                    if attn and u == 2:
                        pe.wait_ge(qk_ready, 2 * g + 2)
                        pe.wait_ge(tile_out, T_FOX + 4 * g + 4)
                        for t in range(TB):
                            n = (t + 1) * P
                            dst = {0: bank[6][:, 384:512], 1: bank[7][:, 0:256],
                                   2: bank[6][:, 0:384], 3: bank[5][:, :]}[t]
                            ins = pe.matmul(dst, q_t[:, t * P:n], k_t[:, 0:n], start=True, stop=True)
                        ins.then_inc(scores_done, 1)
                    if attn and u == 5:
                        pe.wait_ge(probs_ready, g + 1)
                        pe.wait_ge(vtok_ready, g + 1)
                        dsts = [bank[2][:, :], bank[3][:, 0:384], bank[4][:, 0:256], bank[3][:, 384:512]]
                        for kb in range(TB):
                            for t in range(kb, TB):
                                at = prob_at[t] + kb * P
                                ins = pe.transpose(dsts[kb][:, (t - kb) * P:(t - kb + 1) * P],
                                                   prob[:, at:at + P], ident[:, :])
                        ins.then_inc(pt_done, 1)
                    if attn and u == 6:
                        pe.wait_ge(pt_ready, g + 1)
                        for kb in range(TB):
                            n = S - kb * P
                            ins = pe.matmul(bank[5][:, kb * P:S], vtok[:, kb * P:(kb + 1) * P],
                                            probT[:, probT_at[kb]:probT_at[kb] + n],
                                            start=(kb == 0), stop=(kb == TB - 1))
                        ins.then_inc(pv_done, 1)

            def hg_head(h, proj=True, attn=True, first=False, fill=None):
                g = h - 1

                def level(lv):
                    n = 1 << lv
                    nb = P // (2 * n)
                    pe.wait_ge(kmix_ready, LEVELS * g + lv + 1)
                    pe.wait_ge(level_ready, (LEVELS + 1) * g + lv + 1)
                    if lv >= 2:
                        pe.wait_ge(att_ready, LEVELS * g + lv - 1)
                    for pair in range(TB // 2):
                        at = 2 * P * pair
                        queries = bass.AP(q_t.tensor, q_t.offset + at + n,
                                          [list(q_t.ap[0]), [P - n, 2], [2 * n, nb], [1, n]])
                        ins = pe.matmul(bank[2 + lv % 2][:, pair * P:(pair + 1) * P], kmix[:, pair], queries,
                                        start=True, stop=True)
                    ins.then_inc(level_done, 1)

                def slot(n):
                    if n == 0:
                        pe.wait_ge(tile_out, N_HG + 4 * g + 1)
                        turn(bank[4], v_t, TB).then_inc(hg_vt, 1)
                        pe.wait_ge(hg_qk, g + 1)
                        for t in range(TB):
                            c = slice(t * P, (t + 1) * P)
                            ins = pe.matmul(bank[5][:, c], k_t[:, c], q_t[:, c], start=True, stop=True)
                        ins.then_inc(diag_done, 1)
                    if 1 <= n <= LEVELS:
                        level(n - 1)
                    if n == 8:
                        pe.wait_ge(level_ready, (LEVELS + 1) * (g + 1))
                        pe.wait_ge(hg_vtok, g + 1)
                        turn(bank[4], k_t, TB - 1).then_inc(kst_done, 1)
                    if n == 9:
                        pe.wait_ge(kst_ready, g + 1)
                        for t in range(TB - 1):
                            c = slice(t * P, (t + 1) * P)
                            ins = pe.matmul(bank[5][:, c], kst[:, c], vtok[:, c], start=True, stop=True)
                        ins.then_inc(u_done, 1)
                    if n == 10:
                        pe.wait_ge(state_ready, g + 1)
                        pe.wait_ge(att_ready, LEVELS * (g + 1))
                        for t in range(TB):
                            c = slice(t * P, (t + 1) * P)
                            ins = pe.matmul(bank[6][:, c], vtok[:, c], att[:, c], start=True, stop=(t == 0))
                            if t:
                                ins = pe.matmul(bank[6][:, c], st[:, (t - 1) * P:t * P], q_t[:, c],
                                                start=False, stop=True)
                        ins.then_inc(ot_done, 1)
                    if n == 12:
                        pe.wait_ge(osq_ready, g + 1)
                        pe.matmul(bank[7][:, :], ones[:, :], osq, start=True, stop=True).then_inc(ostat_done, 1)

                for u in range(4 * UPT):
                    if attn:
                        slot(2 * u)
                    if proj:
                        j = u // UPT
                        unit(U_HG + u, h, 4 * UPT, T_HG + j, N_HG + 4 * h + j, u % UPT,
                             stage=3 if first and j == 0 else None,
                             mid=(lambda u=u: slot(2 * u + 1)) if attn else None)
                    elif attn:
                        fill(2 * u)
                        slot(2 * u + 1)
                        fill(2 * u + 1)
                    if first and u == 1:
                        sum_squares(2)

            for lay, head in enumerate((fox_head, hg_head)):
                head(0, attn=False, first=True)
                loop(pe, 1, H, head)

                def fill(n, lay=lay):
                    for m, b0, b1 in (FOX_FILL, HG_FILL)[lay].get(n, []):
                        if (m, b0) == (1, 0):
                            pe.wait_ge(tile_out, (T_FOX, N_HG)[lay] + 4 * H)
                        piece(U_OUT[lay], [T_OUT[lay] % 2, T_OUT[lay] % 2 ^ 1], 3 * lay + 1, m, b0, b1)
                head(H, proj=False, fill=fill)
                for m in (2, 3):
                    piece(U_OUT[lay], [T_OUT[lay] % 2, T_OUT[lay] % 2 ^ 1], 3 * lay + 1, m, UB - 1, UB)

                def out_pair(i, lay=lay):
                    for j in range(2):
                        for half in range(UPT):
                            unit(U_OUT[lay] + UPT * j + half, i, 2 * UPT, T_OUT[lay] + j,
                                 2 * i + j + KT * lay, half, freed=yo_ready)
                loop(pe, 1, KT // 2, out_pair)
                sum_squares(2 * lay + 1)

                for m in (0, 2):
                    for b in range(UB):
                        for j in range(2):
                            piece(U_PG[lay], GATE_BANKS, 3 * lay + 2, m + j, b, b + 1)

                def gate_pair(i, lay=lay):
                    for j in range(2):
                        k = 2 * i + j
                        for half in range(UPT):
                            unit(U_PG[lay] + UPT * j + half, i, 2 * UPT, T_PG[lay] + j,
                                 k + KT * lay, half, freed=tg_ready)
                            if lay:
                                if isinstance(i, int) and j == 0:
                                    turn_out(half, half)
                                elif half == 0:
                                    turn_out(k - 1, 1 - j)

                def turn_out(k, slot):
                    pe.wait_ge(h_new, KT + k + 1)
                    wait(pe, out_staged, k - 1)
                    turn(bank[2 + slot], hout2[slot], TB).then_inc(outT_done, 1)
                if lay == 0:
                    loop(pe, 1, KT // 2, gate_pair)
                else:
                    gate_pair(1)
                    loop(pe, 2, KT // 2, gate_pair)
                    turn_out(KT - 1, 1)


_INS = ["x", "p", "w_in_fox", "b_f_fox", "g_q_fox", "g_k_fox", "w_out_fox", "w_in_hg", "lb_logits", "g_o_hg",
        "w_out_hg", "pre_norm", "post_norm", "w_pe", "w_pg"]


def kernel(**inputs):
    import numpy as _np
    import concourse.bacc as _bacc
    from concourse import mybir as _mybir
    from concourse.bass_utils import run_bass_kernel_spmd as _run

    ident = _np.eye(P, dtype=_np.float32)
    causal = _np.where(_np.arange(P)[None, :] <= _np.arange(P)[:, None], 0.0, NEG).astype(_np.float32)
    levels = _np.zeros((P, LEVELS, 2, P // 2), _np.float32)
    for lv in range(LEVELS):
        n = 1 << lv
        s = _np.arange(P)[:, None]
        b = _np.arange(P // 2)[None, :] // n
        for x in range(2):
            levels[:, lv, x] = (s // (2 * n) == b) & (s // n % 2 == x)
    consts = {"c_ident": ident, "c_causal": causal, "c_levels": levels.reshape(P, -1)}

    nc = _bacc.Bacc("TRN2", target_bir_lowering=False, num_devices=1)
    arrays, args = {}, []
    for name in _INS + list(consts):
        a = consts[name] if name in consts else _np.ascontiguousarray(inputs[name])
        arrays[f"in_{name}_dram"] = a
        args.append(nc.dram_tensor(f"in_{name}_dram", a.shape, _mybir.dt.from_np(a.dtype), kind="ExternalInput").ap())
    args.append(nc.dram_tensor("out_0_dram", (1, S, D), _mybir.dt.float32, kind="ExternalOutput").ap())
    trunk(nc, *args)
    r = _run(nc, [arrays], core_ids=[0])
    return r.results[0]["out_0_dram"]
```

```python
from contextlib import ExitStack

import concourse.bass as bass
from concourse import mybir

F32 = mybir.dt.float32
F32R = mybir.dt.float32r
U8 = mybir.dt.uint8
ALU = mybir.AluOpType
ACT = mybir.ActivationFunctionType
AX = mybir.AxisListType

P = 128
S = 512
D = 2048
KT = D // P
TB = S // P
H = D // P
PLE = 256
PK = PLE // P
EPS = 1e-6
NEG = -1e30
LEVELS = 7

UB = 8
UPT = KT // UB
PE_UNITS = PK * KT // UB
RAW, RING = 2, 4
HI_AHEAD, LO_AHEAD = 3, 2
NORM_LAG = 2
GATE_BANKS = [4, 5]
U_PE = 0
U_F = U_PE + PE_UNITS
U_FOX = U_F + UPT
U_OUT = [U_FOX + 4 * UPT * H, 0]
EM_UNITS = PE_UNITS // 2 + 1
U_EM = [U_OUT[0] + UPT * KT, 0]
U_PG = [U_EM[0] + EM_UNITS, 0]
U_HG = U_PG[0] + UPT * KT
U_OUT[1] = U_HG + 4 * UPT * H
U_EM[1] = U_OUT[1] + UPT * KT
U_PG[1] = U_EM[1] + EM_UNITS
U_END = U_PG[1] + UPT * KT

T_PE = 0
T_F = T_PE + KT
T_FOX = T_F + 1
T_OUT = [T_FOX + 4 * H, 0]
T_PG = [T_OUT[0] + KT, 0]
T_HG = T_PG[0] + KT
T_OUT[1] = T_HG + 4 * H
T_PG[1] = T_OUT[1] + KT
N_HG = T_FOX + 4 * H

FOX_FILL = {0: [(m, b, b + 1) for b in range(6) for m in (0, 1)], 3: [(m, b, b + 1) for b in (6, 7) for m in (0, 1)],
            4: [(2, 0, 7)], 5: [(3, 0, 2)], 6: [(3, 2, 5)], 7: [(3, 5, 7)]}
HG_FILL = {0: [(0, 0, 2)], 1: [(0, 2, 4)], 2: [(1, 0, 2)], 3: [(1, 2, 4)],
           4: [(0, 4, 5), (1, 4, 5)], 5: [(0, 5, 6), (1, 5, 6)], 6: [(0, 6, 7), (1, 6, 7)],
           7: [(0, 7, 8), (1, 7, 8)], 8: [(2, 0, 2)], 9: [(2, 2, 5)], 10: [(2, 5, 7), (3, 0, 1)], 12: [(3, 1, 7)]}
FOX_HI = {0: (0, 2, []), 1: (2, 8, [3]), 2: (8, 15, []), 5: (0, 0, [4, 5])}
FOX_LO = {3: [2], 4: [3], 6: [4], 7: [5]}
HG_HI = {0: (0, 6, []), 1: (6, 10, [3]), 2: (10, 15, []), 4: (0, 0, [4]), 5: (0, 0, [5])}
HG_LO = {1: [2], 2: [3], 4: [4], 5: [5]}

G_PRE, G_POST, G_LB, G_Q, G_K, G_O, G_ROWS = 0, 2 * KT, 4 * KT, 6 * KT, 6 * KT + 1, 6 * KT + 2, 6 * KT + 3


def trunk(nc, x, p, w_in_fox, b_f_fox, g_q_fox, g_k_fox, w_out_fox, w_in_hg, lb_logits, g_o_hg,
          w_out_hg, pre_norm, post_norm, w_pe, w_pg, c_ident, c_causal, c_levels, out):
    pe_scr = nc.dram_tensor("pe_scr", (2 * KT, P, S), F32, kind="Internal").ap()
    p_scr = nc.dram_tensor("p_scr", (P, PK, S), F32, kind="Internal").ap()
    c_scr = nc.dram_tensor("c_scr", (H, S), F32, kind="Internal").ap()

    def rows_of(w):
        return w.rearrange("(k p) n -> p k n", p=P)

    wf, wh = rows_of(w_in_fox[0]), rows_of(w_in_hg[0])
    wo = [rows_of(w_out_fox[0]), rows_of(w_out_hg[0])]
    wg = [rows_of(w_pg[i]) for i in range(2)]
    x_tok = x[0].rearrange("(t p) n -> p t n", p=P)
    out_tok = out[0].rearrange("(t p) n -> p t n", p=P)

    ctx = ExitStack()
    with ctx:
        def sb(name, shape, dt=F32):
            return ctx.enter_context(nc.sbuf_tensor(name, shape, dt))

        def sem(name):
            return ctx.enter_context(nc.semaphore(name))

        ctx.enter_context(nc.allow_non_contiguous_dma(reason="one column of forget biases"))

        hT = sb("hT", [P, KT, S])
        xhi = sb("xhi", [P, KT, S], F32R)
        xlo = sb("xlo", [P, KT, S], F32R)
        yT = sb("yT", [P, KT, S])
        raw = sb("raw", [P, RAW, UB * P])
        whi = sb("whi", [P, RING, UB, P], F32R)
        wlo = sb("wlo", [P, RING, UB, P], F32R)
        rinv = sb("rinv", [P, S])
        ident = sb("ident", [P, P])
        ones = sb("ones", [P, P])
        kmix = sb("kmix", [P, TB // 2, P])
        causal = sb("causal", [P, P])
        levels = sb("levels", [P, LEVELS, S // 2], U8)
        gcol = sb("gcol", [P, P])
        lbc = sb("lbc", [P, 6, KT])
        cq = sb("cq", [P, TB, 32])
        small = sb("small", [P, 16])
        eps_c, one_c, bf_c = small[:, 0:1], small[:, 1:2], small[:, 2:3]
        negm, rsum = small[:, 4:8], small[:, 8:12]
        work = sb("work", [P, 15 * S])

        def wk(i, n=1):
            return work[:, i * S:(i + n) * S]

        q_t, k_t, v_t, z_t, tz_t, vtok = wk(0), wk(1), wk(2), wk(3), wk(4), wk(14)
        sqq, sqk, ckb, ckm = wk(5), wk(6), wk(7), wk(8)
        prob, probT = work[:, 9 * S:9 * S + 1280], work[:, 9 * S + 1280:9 * S + 2560]
        prob_at = [0, 128, 384, 768]
        probT_at = [0, 512, 896, 1152]
        osq, f_t, tree, att, kst, st, o_t, tq_t = (wk(i) for i in range(5, 13))
        sq2, acc = [wk(5), wk(6)], wk(13)
        tg2, pe2, hout2, ostage2 = [wk(0), wk(1)], [wk(2), wk(3)], [wk(7), wk(8)], [wk(9), wk(10)]
        xstage = [wk(i) for i in range(4)]
        pstage = [wk(7, 2), wk(9, 2)]
        pe_tile = [wk(12), wk(4), wk(14), wk(7)]
        embed_banks = [0, 1, 4, 5]
        p_turned, later_banks = yT[:, 4:4 + PK], [2, 3, 6, 0]
        em_tile = [wk(i) for i in (0, 1, 4, 9, 10, 11, 12, 14)]
        grow, level_in = yT[:, 0, 0:P], yT[:, 1:3].rearrange("p a n -> p (a n)")[:, 0:LEVELS * P]
        fl, fa, fc, fone = wk(7), wk(8), wk(9), wk(10)
        FR = slice(P - 32, P)

        bank = [ctx.enter_context(nc.psum_tensor(f"bank{i}", [P, S], F32)) for i in range(8)]

        w_loaded = [sem(f"w_loaded{i}") for i in range(RAW)]
        hi_done, lo_done, w_used = sem("hi_done"), sem("lo_done"), sem("w_used")
        embed_done, tile_out = sem("embed_done"), sem("tile_out")
        xhi_done, x_ready = sem("xhi_done"), sem("x_ready")
        acc_zero, sq_done, acc_step = sem("acc_zero"), sem("sq_done"), sem("acc_step")
        norm_done, norm_rms, norm_ready = sem("norm_done"), sem("norm_rms"), sem("norm_ready")
        y_ready, yo_ready, yn_ready, hn_ready = sem("y_ready"), sem("yo_ready"), sem("yn_ready"), sem("hn_ready")
        tg_ready, h_new = sem("tg_ready"), sem("h_new")
        ident_in, gvec_in, const_in, const_set, bias_in = (
            sem(n) for n in ("ident_in", "gvec_in", "const_in", "const_set", "bias_in"))
        p_in = [sem("p_in0"), sem("p_in1")]
        pt_p, phi_done, p_ready = sem("p_turned"), sem("phi_done"), sem("p_ready")
        p_staged, p_saved = sem("p_staged"), sem("p_saved")
        em_out, em_stored = sem("em_out"), sem("em_stored")
        x_in = [sem(f"x_in{i}") for i in range(4)]
        x_turned, h_ready = sem("x_turned"), sem("h_ready")
        g_turned, g_ready = sem("g_turned"), sem("g_ready")
        lb_sem, lb_exp = sem("lb_step"), sem("lb_exp")
        pe_stored = [sem(f"pe_stored{i}") for i in range(4)]
        pe_in = [sem("pe_in0"), sem("pe_in1")]
        f_pre, f_exp, f_ln, f_cum, f_turned, cq_ready, c_stored = (
            sem(n) for n in ("f_pre", "f_exp", "f_ln", "f_cum", "f_turned", "cq_ready", "c_stored"))
        sq_ready, stats_done, rms_ready, qk_ready = sem("sq_ready"), sem("stats_done"), sem("rms_ready"), sem("qk_ready")
        vt_done, vtok_ready, tz_ready, zs_ready = sem("vt_done"), sem("vtok_ready"), sem("tz_ready"), sem("zs_ready")
        ck_in, ckm_ready = sem("ck_in"), sem("ckm_ready")
        scores_done, negm_ready, exp_ready = sem("scores_done"), sem("negm_ready"), sem("exp_ready")
        probs_ready, pt_done, pt_ready, pv_done = sem("probs_ready"), sem("pt_done"), sem("pt_ready"), sem("pv_done")
        hg_vt, hg_vtok, hg_tz = sem("hg_vt"), sem("hg_vtok"), sem("hg_tz")
        hg_qk, diag_done, level_ready, level_done, att_ready = (
            sem(n) for n in ("hg_qk", "diag_done", "level_ready", "level_done", "att_ready"))
        kst_done, kst_ready, u_done, state_ready = sem("kst_done"), sem("kst_ready"), sem("u_done"), sem("state_ready")
        ot_done, o_ready, osq_ready, ostat_done, orms_ready = (
            sem(n) for n in ("ot_done", "o_ready", "osq_ready", "ostat_done", "orms_ready"))
        thf_ready, tq_ready = sem("thf_ready"), sem("tq_ready")
        keys_ready, kmix_ready = sem("keys_ready"), sem("kmix_ready")
        outT_done, out_staged = sem("outT_done"), sem("out_staged")
        out_stored = [sem("out_stored0"), sem("out_stored1")]
        v_step = sem("v_step")

        def wait(eng, s, value):
            if not (isinstance(value, int) and value <= 0):
                eng.wait_ge(s, value)

        def end_of(k):
            return 2 * UPT - 1 if isinstance(k, int) and k == 0 else UPT * k + UPT

        def loop(eng, first, last, body):
            with eng.Fori(first, last) as i:
                body(i)

        block = ctx.enter_context(nc.Block())

        @block.sync
        def _(sp):
            def load(u, i, per, src, k=UB):
                n = u + per * i
                if not isinstance(n, int) or n >= RAW:
                    sp.wait_ge(lo_done, n - RAW + 1)
                dst = raw[:, u % RAW, :].rearrange("p (k n) -> p k n", k=k)
                sp.dma_start(dst, src).then_inc(w_loaded[u % RAW], 16)

            def tile_units(u, i, per, w, col):
                for j in range(UPT):
                    load(u + j, i, per, w[:, UB * j:UB * (j + 1), bass.ds(col, P)])

            sp.dma_start(ident[:, :], c_ident).then_inc(ident_in, 16)
            for dst, src in ((grow[G_PRE:G_PRE + 2 * KT, :], pre_norm.rearrange("l (k p) -> (l k) p", p=P)),
                             (grow[G_POST:G_POST + 2 * KT, :], post_norm.rearrange("l (k p) -> (l k) p", p=P)),
                             (grow[G_LB:G_LB + 2 * KT, :], lb_logits.rearrange("l (k p) -> (l k) p", p=P)),
                             (grow[G_Q:G_Q + 1, :], g_q_fox), (grow[G_K:G_K + 1, :], g_k_fox),
                             (grow[G_O:G_O + 1, :], g_o_hg)):
                sp.dma_start(dst, src).then_inc(gvec_in, 16)
            we = [rows_of(w_pe[i]) for i in range(2)]

            def first_units(*units):
                for u in units:
                    if u < U_F:
                        load(u, 0, 0, we[0][:, :, 4 * P * u:4 * P * (u + 1)], k=PK)
                    else:
                        k = UB * (u - U_F)
                        load(u, 0, 0, wf[:, k:k + UB, 4 * D + H - P:4 * D + H])

            def load_x(first):
                for k in range(first, first + 4):
                    if k >= 4:
                        sp.wait_ge(x_turned, k - 3)
                    sp.dma_start(xstage[k % 4].rearrange("p (t n) -> p t n", t=TB),
                                 x_tok[:, :, k * P:(k + 1) * P]).then_inc(x_in[k % 4], 16)
            first_units(0)
            load_x(0)
            first_units(1, 2, 3)
            first_units(U_F)
            load_x(4)
            first_units(U_F + 1)
            load_x(8)
            load_x(12)

            def fox_head(n):
                for j in range(4):
                    tile_units(U_FOX + UPT * j, n - 1, 4 * UPT, wf, n * P + (j * D - P))

            def hg_head(n):
                for j, part in enumerate((2, 1, 0, 3)):
                    tile_units(U_HG + UPT * j, n - 1, 4 * UPT, wh, n * P + (part * D - P))

            def later_embed(lay):
                for a in range(EM_UNITS - 1):
                    j = (EM_UNITS - 1) * lay + a
                    load(U_EM[lay] + a, 0, 0, we[1][:, :, 4 * P * j:4 * P * (j + 1)], k=PK)
                sp.wait_ge(p_saved, 16)
                load(U_EM[lay] + EM_UNITS - 1, 0, 0, p_scr, k=PK)
                for j in range(2):
                    load(U_PG[lay] + j, 0, 0, wg[lay][:, 0:UB, j * P:(j + 1) * P])
                for n in range(KT // 2):
                    sp.wait_ge(em_out, KT // 2 * lay + n + 1)
                    sp.dma_start(pe_scr[KT + KT // 2 * lay + n], em_tile[n]).then_inc(em_stored, 16)

            def square(u, w, skip=0):
                def pair(i):
                    for j in range(2):
                        tile_units(u + UPT * j, i, 2 * UPT, w, (2 * i + j) * P)
                for m in range(skip, 2 * UPT):
                    half, j = m // 2, m % 2
                    load(u + m, 0, 0, w[:, UB * half:UB * (half + 1), j * P:(j + 1) * P])
                loop(sp, 2, KT // 2 + 1, lambda i: pair(i - 1))

            loop(sp, 1, H + 1, fox_head)
            square(U_OUT[0], wo[0])
            later_embed(0)
            square(U_PG[0], wg[0], skip=2)
            loop(sp, 1, H + 1, hg_head)
            square(U_OUT[1], wo[1])
            later_embed(1)
            square(U_PG[1], wg[1], skip=2)

        @block.gpsimd
        def _(pool):
            for i in range(2):
                pool.dma_start(pstage[i].rearrange("p (t n) -> p t n", t=TB),
                               p[i, 0].rearrange("(t p) n -> p t n", p=P)).then_inc(p_in[i], 16)

            for dst, src in ((causal[:, :], c_causal), (level_in, c_levels)):
                pool.dma_start(dst, src).then_inc(const_in, 16)
            pool.wait_ge(const_set, 1)
            pool.dma_start(bf_c[P - H:P, :], b_f_fox.rearrange("a h -> h a")).then_inc(bias_in, 16)

            pool.wait_ge(p_staged, PK)
            pool.dma_start(p_scr, p_turned).then_inc(p_saved, 16)
            for n in range(KT):
                pool.wait_ge(tile_out, n + 1)
                pool.dma_start(pe_scr[n], pe_tile[n % 4]).then_inc(pe_stored[n % 4], 16)

            pool.wait_ge(f_cum, 1)
            pool.dma_start(c_scr, fc[P - H:P, :]).then_inc(c_stored, 16)
            pool.wait_ge(c_stored, 16)

            def decay_row(g):
                if not isinstance(g, int):
                    pool.wait_ge(negm_ready, TB * g)
                pool.dma_start(ckb, c_scr[bass.ds(g, 1), :].to_broadcast([P, S])).then_inc(ck_in, 16)
                pool.wait_ge(ck_in, 16 * g + 16)
                pool.tensor_tensor(ckm.rearrange("p (t n) -> p t n", t=TB),
                                   ckb.rearrange("p (t n) -> p t n", t=TB),
                                   causal[:, :].unsqueeze(1).to_broadcast([P, TB, P]),
                                   ALU.subtract).then_inc(ckm_ready, 1)
            pool.wait_ge(const_in, 32)
            pool.wait_ge(f_ln, 2)
            pool.wait_ge(cq_ready, 1)
            decay_row(0)
            loop(pool, 1, H, decay_row)

            for lay in range(2):
                def split_y(k, lay=lay):
                    pool.wait_ge(xhi_done, KT * (3 * lay + 1) + k + 1)
                    pool.tensor_tensor(xlo[:, k], yT[:, k], xhi[:, k].bitcast(F32),
                                       ALU.subtract).then_inc(x_ready, 1)
                loop(pool, 0, KT - 1, split_y)

                def split_gate(m, lay=lay):
                    u = U_PG[lay] + m
                    pool.wait_ge(lo_done, u)
                    pool.wait_ge(hi_done, u + 1)
                    pool.wait_ge(w_used, u - RING + 1)
                    pool.tensor_tensor(wlo[:, u % RING].rearrange("p k n -> p (k n)"), raw[:, u % RAW, :],
                                       whi[:, u % RING].rearrange("p k n -> p (k n)").bitcast(F32),
                                       ALU.subtract).then_inc(lo_done, 1)
                split_gate(0)
                split_gate(1)

                def add_h(k, lay=lay):
                    pool.wait_ge(yn_ready, KT * lay + k + 1)
                    pool.tensor_tensor(hT[:, k], hT[:, k], yT[:, k], ALU.add).then_inc(hn_ready, 1)
                loop(pool, 0, KT, add_h)

                def load_pe(i, lay=lay):
                    for j in range(2):
                        if not isinstance(i, int):
                            pool.wait_ge(h_new, KT * lay + 2 * i + j - 1)
                        pool.dma_start(pe2[j], pe_scr[KT * lay + 2 * i + j]).then_inc(pe_in[j], 16)

                def store_out(i):
                    for j in range(2):
                        pool.wait_ge(out_staged, 2 * i + j + 1)
                        pool.dma_start(out_tok[:, :, bass.ds((2 * i + j) * P, P)],
                                       ostage2[j].rearrange("p (t n) -> p t n", t=TB)).then_inc(out_stored[j], 16)
                if lay == 0:
                    for j in range(4):
                        pool.wait_ge(pe_stored[j], 16 * (KT // 4))
                else:
                    pool.wait_ge(em_stored, 16 * KT)
                load_pe(0)
                if lay == 0:
                    loop(pool, 1, KT // 2, load_pe)
                else:
                    def turn(i):
                        load_pe(i)
                        store_out(i - 1)
                    loop(pool, 1, KT // 2, turn)
                    store_out(KT // 2 - 1)
            for j in range(2):
                pool.wait_ge(out_stored[j], 16 * KT // 2)

        @block.scalar
        def _(act):
            def split(u, i=0, per=0):
                n = u + per * i
                if isinstance(n, int) and n >= U_END:
                    return
                act.wait_ge(w_loaded[u % RAW], 16 * (u // RAW + 1) + (16 * per // RAW) * i)
                wait(act, w_used, n - RING + 1)
                act.activation(whi[:, u % RING].rearrange("p k n -> p (k n)"), raw[:, u % RAW, :],
                               ACT.Copy).then_inc(hi_done, 1)

            def split_h(lay, first, last, scaled=False):
                def one(k):
                    if not scaled:
                        act.wait_ge(hn_ready, KT * lay + k + 1)
                    scale = gcol[:, bass.ds(G_PRE + KT + k, 1)] if scaled else 1.0
                    act.activation(xhi[:, k], hT[:, k], ACT.Copy, scale=scale).then_inc(xhi_done, 1)
                if last - first == 1:
                    one(first)
                else:
                    loop(act, first, last, one)

            def split_y(lay, k):
                act.wait_ge(y_ready, KT * lay + k + 1)
                act.activation(xhi[:, k], yT[:, k], ACT.Copy).then_inc(xhi_done, 1)

            def token_rms(stage):
                act.wait_ge(norm_done, stage + 1)
                act.activation(rinv[:, :], bank[7][:, :], ACT.Sqrt, bias=eps_c, scale=1.0 / D).then_inc(norm_rms, 1)

            for n in range(PK):
                act.wait_ge(pt_p, n + 1)
                act.activation(xhi[:, KT - PK + n], bank[2 + n][:, :], ACT.Copy).then_inc(phi_done, 1)
            split(0)
            for n in range(PK):
                act.wait_ge(pt_p, PK + n + 1)
                act.activation(p_turned[:, n], bank[2 + PK + n][:, :], ACT.Copy).then_inc(p_staged, 1)
            act.wait_ge(g_turned, 1)
            act.activation(gcol[:, 0:G_ROWS], bank[7][:, 0:G_ROWS], ACT.Copy).then_inc(g_ready, 1)
            for u in range(1, HI_AHEAD):
                split(u)
            act.wait_ge(p_ready, PK)

            def take_x(k, slot):
                act.wait_ge(x_turned, k + 1)
                act.activation(hT[:, k], bank[2 + slot][:, :], ACT.Copy).then_inc(h_ready, 1)
                wait(act, acc_step, k - 1)
                act.activation(sq2[slot], bank[2 + slot][:, :], ACT.Square).then_inc(sq_done, 1)

            def split_x(k):
                act.wait_ge(h_ready, k + 1)
                act.activation(xhi[:, k], hT[:, k], ACT.Copy,
                               scale=gcol[:, G_PRE + k:G_PRE + k + 1]).then_inc(xhi_done, 1)
            for u in range(PE_UNITS):
                for m in range(4):
                    take_x(4 * u + m, m % 2)
                    if m % 2:
                        split_x(2 * u + m // 2)
                    if m == 1:
                        split(U_PE + u + HI_AHEAD)
            for k in range(2 * PE_UNITS, KT):
                if k == KT - PK:
                    act.wait_ge(w_used, U_F)
                split_x(k)
            split(U_F + HI_AHEAD)
            token_rms(0)
            split(U_F + 1 + HI_AHEAD)
            act.wait_ge(lb_sem, 2)
            act.activation(lbc[:, 0:2], lbc[:, 0:2], ACT.Exp).then_inc(lb_exp, 1)
            act.wait_ge(f_pre, 1)
            act.activation(fa[FR, :], fl[FR, :], ACT.Abs).then_inc(f_exp, 1)
            act.wait_ge(f_exp, 1)
            act.activation(fa[FR, :], fa[FR, :], ACT.Exp, scale=-1.0).then_inc(f_exp, 1)
            act.wait_ge(f_exp, 2)
            act.activation(fa[FR, :], fa[FR, :], ACT.Ln, bias=one_c[FR, :]).then_inc(f_ln, 1)

            def fox_head(h, proj=True, attn=True, first=False, fill=None):
                g = h - 1
                for u in range(4 * UPT):
                    if proj:
                        split(U_FOX + u + HI_AHEAD, h, 4 * UPT)
                    elif fill is not None:
                        fill(u)
                    if first and u == 4:
                        act.wait_ge(f_turned, 1)
                        act.activation(cq[:, :, :], bank[6][:, 0:TB * 32].rearrange("p (t n) -> p t n", t=TB),
                                       ACT.Copy).then_inc(cq_ready, 1)
                        for n in range(4):
                            act.wait_ge(pe_stored[n], 16 * (KT // 4))
                    if attn and u == 0:
                        act.wait_ge(stats_done, 2 * g + 1)
                        act.activation(sqq, bank[2][:, :], ACT.Sqrt, bias=eps_c, scale=1.0 / P).then_inc(rms_ready, 1)
                        act.wait_ge(stats_done, 2 * g + 2)
                        act.activation(sqk, bank[3][:, :], ACT.Sqrt, bias=eps_c, scale=1.0 / P).then_inc(rms_ready, 1)
                    if attn and u == 2:
                        act.wait_ge(vt_done, g + 1)
                        act.activation(vtok, bank[4][:, :], ACT.Copy).then_inc(vtok_ready, 1)
                        act.wait_ge(tile_out, T_FOX + 4 * g + 4)
                        act.activation(tz_t, z_t, ACT.Tanh).then_inc(tz_ready, 1)
                    if attn and u == 4:
                        for t in range(TB):
                            pr = prob[:, prob_at[t]:prob_at[t] + (t + 1) * P]
                            act.wait_ge(negm_ready, TB * g + t + 1)
                            act.activation(pr, pr, ACT.Exp, bias=negm[:, t:t + 1],
                                           accum_out=rsum[:, t:t + 1]).then_inc(exp_ready, 1)
                    if attn and u == 6:
                        act.wait_ge(pt_done, g + 1)
                        act.activation(probT[:, 0:512], bank[2][:, :], ACT.Copy)
                        act.activation(probT[:, 512:896], bank[3][:, 0:384], ACT.Copy)
                        act.activation(probT[:, 1152:1280], bank[3][:, 384:512], ACT.Copy)
                        act.activation(probT[:, 896:1152], bank[4][:, 0:256], ACT.Copy).then_inc(pt_ready, 1)
                    if proj and u == 4:
                        act.wait_ge(tile_out, T_FOX + 4 * h + 1)
                        act.activation(sqq, q_t, ACT.Square).then_inc(sq_ready, 1)
                    if proj and u == 5:
                        act.wait_ge(tile_out, T_FOX + 4 * h + 2)
                        act.activation(sqk, k_t, ACT.Square).then_inc(sq_ready, 1)

            def mix_keys(lv, g):
                n = 1 << lv
                act.wait_ge(keys_ready, (LEVELS + 1) * g + lv + 1)
                for pair in range(TB // 2):
                    keys = bass.AP(k_t.tensor, k_t.offset + 2 * P * pair,
                                   [list(k_t.ap[0]), [2 * n, P // (2 * n)], [P + n, 2], [1, n]])
                    ins = act.activation(kmix[:, pair].rearrange("p (b e n) -> p b e n", e=2, n=n), keys, ACT.Copy)
                ins.then_inc(kmix_ready, 1)

            def hg_head(h, proj=True, attn=True, first=False, fill=None):
                g = h - 1
                for u in range(4 * UPT):
                    if proj:
                        split(U_HG + u + HI_AHEAD, h, 4 * UPT)
                    elif fill is not None:
                        fill(u)
                    if first and u == 2:
                        token_rms(2)
                    if attn and u == 0:
                        act.wait_ge(hg_vt, g + 1)
                        act.activation(vtok, bank[4][:, :], ACT.Copy).then_inc(hg_vtok, 1)
                    if attn and 1 <= u < 4:
                        mix_keys(2 * u, g)
                    if attn and u < 3:
                        mix_keys(2 * u + 1, g)
                    if attn and u == 2:
                        act.wait_ge(tile_out, N_HG + 4 * g + 4)
                        act.activation(tz_t, z_t, ACT.Tanh).then_inc(hg_tz, 1)
                    if attn and u == 4:
                        act.wait_ge(kst_done, g + 1)
                        act.activation(kst[:, 0:3 * P], bank[4][:, 0:3 * P], ACT.Copy).then_inc(kst_ready, 1)
                    if proj and u == 5:
                        act.wait_ge(tile_out, N_HG + 4 * h + 2)
                        act.activation(f_t, f_t, ACT.Tanh, scale=0.5).then_inc(thf_ready, 1)
                    if attn and u == 5:
                        act.wait_ge(o_ready, g + 1)
                        act.activation(osq, o_t, ACT.Square).then_inc(osq_ready, 1)
                    if attn and u == 6:
                        act.wait_ge(ostat_done, g + 1)
                        act.activation(osq, bank[7][:, :], ACT.Sqrt, bias=eps_c, scale=1.0 / P).then_inc(orms_ready, 1)
                    if proj and u == 6:
                        mix_keys(0, h)
                    if proj and u == 7:
                        act.wait_ge(tile_out, N_HG + 4 * h + 3)
                        act.activation(tq_t, q_t, ACT.Tanh).then_inc(tq_ready, 1)

            for lay, head in enumerate((fox_head, hg_head)):
                head(0, attn=False, first=True)
                loop(act, 1, H, head)
                def fill(u, lay=lay):
                    first, last, units = (FOX_HI, HG_HI)[lay].get(u, (0, 0, []))
                    for k in range(first, last):
                        split_y(lay, k)
                    for m in units:
                        split(U_OUT[lay] + m)
                act.wait_ge(w_used, U_OUT[lay])
                head(H, proj=False, fill=fill)
                split_y(lay, KT - 1)
                split(U_OUT[lay] + 2 * UPT + 2)

                def out_pair(i, lay=lay):
                    for j in range(2):
                        if not (isinstance(i, int) and i == 0):
                            for m in range(UPT):
                                split(U_OUT[lay] + UPT * j + m + HI_AHEAD, i, 2 * UPT)
                        k = 2 * i + j
                        act.wait_ge(yo_ready, KT * lay + k + 1)
                        if not (isinstance(i, int) and i == 0):
                            act.wait_ge(acc_step, (KT - 1) * (2 * lay + 1) + k - 1)
                        act.activation(sq2[j], yT[:, k], ACT.Square).then_inc(sq_done, 1)
                out_pair(0)
                loop(act, 1, KT // 2, out_pair)
                token_rms(2 * lay + 1)
                split(U_PG[lay])

                def take_embed(a, f, lay=lay):
                    if f < 3:
                        act.wait_ge(embed_done, 3 * (PE_UNITS + 2 * lay + a) + f + 1)
                    else:
                        act.wait_ge(w_used, (U_EM[lay] + 1, U_PG[lay])[a])
                    act.activation(em_tile[4 * a + f], bank[later_banks[f]][:, :], ACT.Copy).then_inc(em_out, 1)
                for f in range(4):
                    take_embed(0, f)
                split(U_PG[lay] + 1)
                for f in range(4):
                    take_embed(1, f)
                    if f:
                        split_h(lay, f - 1, f)
                split_h(lay, 3, 6)
                split(U_PG[lay] + 2)
                split_h(lay, 6, 7)
                split(U_PG[lay] + 3)
                split_h(lay, 7, KT - 2)
                for m in (1, 2):
                    split(U_PG[lay] + HI_AHEAD + m)
                    split_h(lay, KT - 3 + m, KT - 2 + m)
                split(U_PG[lay] + HI_AHEAD + 3)

                act.wait_ge(em_stored, 16 * KT // 2 * (lay + 1))

                def gate_pair(i, lay=lay, last=False):
                    for j in range(2):
                        k = 2 * i + j
                        if not (isinstance(i, int) and i == 0):
                            for m in range(UPT):
                                split(U_PG[lay] + UPT * j + m + HI_AHEAD, i, 2 * UPT)
                        act.wait_ge(w_used, U_PG[lay] + end_of(k))
                        if not (isinstance(i, int) and i == 0):
                            act.wait_ge(h_new, KT * lay + k - 1)
                        if last and j == 1:
                            split_h(lay, 0, 1, scaled=True)
                        src = bank[GATE_BANKS[j] if isinstance(i, int) and i == 0 else T_PG[lay] % 2 ^ j]
                        act.activation(tg2[j], src[:, :], ACT.Tanh, scale=0.5).then_inc(tg_ready, 1)
                        if last and j == 1:
                            split_h(lay, 1, 3, scaled=True)
                        if lay == 0:
                            act.wait_ge(h_new, k + 1)
                            if not (isinstance(i, int) and i == 0):
                                act.wait_ge(acc_step, 2 * (KT - 1) + k - 1)
                            act.activation(sq2[j], hT[:, k], ACT.Square).then_inc(sq_done, 1)
                        elif not (isinstance(k, int) and k == 0):
                            stage_out(k - 1, 1 - j)

                def stage_out(k, slot):
                    act.wait_ge(outT_done, k + 1)
                    if not isinstance(k, int):
                        if slot == 0:
                            act.wait_ge(out_stored[0], 8 * k)
                        else:
                            act.wait_ge(out_stored[1], 8 * k - 8)
                    elif k >= 2:
                        act.wait_ge(out_stored[slot], 16 * (k // 2))
                    act.activation(ostage2[slot], bank[2 + slot][:, :], ACT.Copy).then_inc(out_staged, 1)

                gate_pair(0)
                if lay == 0:
                    loop(act, 1, KT // 2 - 1, gate_pair)
                    gate_pair(KT // 2 - 1, last=True)
                    split_h(lay, 3, KT, scaled=True)
                else:
                    gate_pair(1)
                    loop(act, 2, KT // 2 - 1, gate_pair)
                    gate_pair(KT // 2 - 1)
                    stage_out(KT - 1, 1)

        @block.vector
        def _(dve):
            steps = {"fixed": 0, "turn": None}

            def link(ins):
                ins.then_inc(v_step, 1)
                steps["fixed"] += 1
                turn = steps["turn"]
                dve.wait_ge(v_step, steps["fixed"] if turn is None else steps["fixed"] + turn)

            def linked_loop(first, last, links, body):
                start = steps["fixed"]
                with dve.Fori(first, last) as i:
                    steps["turn"] = links * (i - first)
                    body(i)
                    steps["turn"] = None
                assert steps["fixed"] == start + links, steps["fixed"] - start
                steps["fixed"] = start + links * (last - first)

            def split(u, i=0, per=0):
                n = u + per * i
                if isinstance(n, int) and n >= U_END:
                    return
                dve.wait_ge(hi_done, n + 1)
                wait(dve, w_used, n - RING + 1)
                dve.tensor_tensor(wlo[:, u % RING].rearrange("p k n -> p (k n)"), raw[:, u % RAW, :],
                                  whi[:, u % RING].rearrange("p k n -> p (k n)").bitcast(F32),
                                  ALU.subtract).then_inc(lo_done, 1)

            def split_one(stage, src, k):
                dve.wait_ge(xhi_done, KT * stage + k + 1)
                dve.tensor_tensor(xlo[:, k], src[:, k], xhi[:, k].bitcast(F32), ALU.subtract).then_inc(x_ready, 1)

            def split_scaled(stage, scale_at, first, last):
                def one(k):
                    dve.wait_ge(xhi_done, KT * stage + k + 1)
                    dve.scalar_tensor_tensor(xlo[:, k], hT[:, k], gcol[:, bass.ds(scale_at + k, 1)],
                                             xhi[:, k].bitcast(F32), ALU.mult, ALU.subtract).then_inc(x_ready, 1)
                loop(dve, first, last, one)

            def zero_acc():
                link(dve.memset(acc, 0.0))

            def add_square(k, stage, slot):
                if isinstance(k, int) and k == KT - 1:
                    return
                dve.wait_ge(sq_done, KT * stage + k + 1)
                wait(dve, acc_step, (KT - 1) * stage + k)
                dve.tensor_tensor(acc, acc, sq2[slot], ALU.add).then_inc(acc_step, 1)

            def token_rinv(stage):
                dve.wait_ge(norm_rms, stage + 1)
                dve.reciprocal(rinv[:, :], rinv[:, :]).then_inc(norm_ready, 1)
                dve.wait_ge(norm_ready, stage + 1)

            def take_tile(t0, used, dst, halve=False):
                dve.wait_ge(w_used, used)
                src = bank[t0 % 2][:, :]
                if halve:
                    dve.scalar_tensor_tensor(dst, src, 0.5, rinv[:, :], ALU.mult, ALU.mult).then_inc(tile_out, 1)
                else:
                    dve.tensor_tensor(dst, src, rinv[:, :], ALU.mult).then_inc(tile_out, 1)

            def reversed_chunks(tile):
                return chunks(tile, 1)[:, :, ::-1]

            def chunks(tile, x):
                return tile.rearrange("p (a x n) -> p a x n", x=2, n=P)[:, :, x]

            def take_hg_tile(t0, used, dst, halve=False):
                dve.wait_ge(w_used, used)
                for x in range(2):
                    to = reversed_chunks(dst) if x else chunks(dst, x)
                    src, r = chunks(bank[t0 % 2][:, :], x), chunks(rinv[:, :], x)
                    if halve:
                        ins = dve.scalar_tensor_tensor(to, src, 0.5, r, ALU.mult, ALU.mult)
                    else:
                        ins = dve.tensor_tensor(to, src, r, ALU.mult)
                ins.then_inc(tile_out, 1)

            dve.memset(small[:, 2:3], 0.0)
            dve.memset(ones[:, :], 1.0).then_inc(const_set, 1)
            dve.memset(eps_c, EPS)
            dve.memset(one_c, 1.0)
            dve.memset(acc, 0.0)
            link(dve.memset(small[:, 3:4], 0.0))
            for n in range(PK):
                dve.wait_ge(phi_done, n + 1)
                dve.tensor_tensor(xlo[:, KT - PK + n], bank[2 + n][:, :],
                                  xhi[:, KT - PK + n].bitcast(F32), ALU.subtract).then_inc(p_ready, 1)
            for u in range(LO_AHEAD):
                split(u)
            dve.wait_ge(g_ready, 1)
            link(dve.tensor_scalar(gcol[:, G_Q:G_Q + 1], gcol[:, G_Q:G_Q + 1], float(P) ** -0.5, None, ALU.mult))
            l0, l1 = gcol[:, G_LB:G_LB + KT], gcol[:, G_LB + KT:G_LB + 2 * KT]
            link(dve.tensor_tensor(lbc[:, 2], l0, l1, ALU.max))
            dve.tensor_tensor(lbc[:, 0], l0, lbc[:, 2], ALU.subtract).then_inc(lb_sem, 1)
            dve.tensor_tensor(lbc[:, 1], l1, lbc[:, 2], ALU.subtract).then_inc(lb_sem, 1)

            def split_h(k):
                dve.wait_ge(xhi_done, k + 1)
                dve.scalar_tensor_tensor(xlo[:, k], hT[:, k], gcol[:, G_PRE + k:G_PRE + k + 1],
                                         xhi[:, k].bitcast(F32), ALU.mult, ALU.subtract).then_inc(x_ready, 1)
            for u in range(PE_UNITS):
                split(U_PE + u + LO_AHEAD)
                for f in range(4):
                    if f < 3:
                        dve.wait_ge(embed_done, 3 * u + f + 1)
                    else:
                        dve.wait_ge(w_used, u + 1)
                    wait(dve, pe_stored[f], 16 * u)
                    dve.tensor_copy(pe_tile[f], bank[embed_banks[f]][:, :]).then_inc(tile_out, 1)
                    if u or f:
                        add_square(4 * u + f - 1, 0, (f - 1) % 2)
                    if f == 0 and u:
                        split_h(2 * u - 1)
                    if f == 2:
                        split_h(2 * u)
            split_h(2 * PE_UNITS - 1)
            for k in range(2 * PE_UNITS, KT):
                split_h(k)
            split(U_F + LO_AHEAD)
            token_rinv(0)
            split(U_F + 1 + LO_AHEAD)
            dve.wait_ge(pe_stored[3], 16 * PE_UNITS)
            link(dve.memset(fone, 1.0))
            dve.wait_ge(w_used, U_F + UPT)
            dve.tensor_tensor(fl[FR, :], bank[T_F % 2][FR, :], rinv[FR, :], ALU.mult).then_inc(tile_out, 1)
            dve.wait_ge(tile_out, T_F + 1)
            dve.wait_ge(bias_in, 16)
            dve.tensor_scalar(fl[FR, :], fl[FR, :], bf_c[FR, :], None, ALU.add).then_inc(f_pre, 1)
            dve.wait_ge(const_in, 32)
            for x in range(2):
                for pair in range(TB // 2):
                    at = (x * TB // 2 + pair) * P // 2
                    ins = dve.tensor_copy(levels[:, :, at:at + P // 2],
                                          level_in.rearrange("p (l x n) -> p l x n", l=LEVELS, x=2)[:, :, x])
            link(ins)
            dve.wait_ge(lb_exp, 1)
            link(dve.tensor_tensor(lbc[:, 2], lbc[:, 0], lbc[:, 1], ALU.add))
            link(dve.reciprocal(lbc[:, 2], lbc[:, 2]))
            dve.tensor_tensor(lbc[:, 3], lbc[:, 0], lbc[:, 2], ALU.mult)
            link(dve.tensor_tensor(lbc[:, 5], lbc[:, 1], lbc[:, 2], ALU.mult))
            link(dve.tensor_tensor(lbc[:, 4], lbc[:, 3], lbc[:, 5], ALU.add))
            link(dve.tensor_tensor(lbc[:, 4], lbc[:, 4], lbc[:, 3], ALU.subtract))
            link(dve.tensor_scalar(lbc[:, 5], lbc[:, 4], -1.0, 1.0, ALU.mult, ALU.add))
            lower, upper = lbc[:, 4], lbc[:, 5]
            dve.wait_ge(f_ln, 1)
            dve.scalar_tensor_tensor(fl[FR, :], fl[FR, :], 0.0, fa[FR, :], ALU.min, ALU.subtract).then_inc(f_ln, 1)
            dve.wait_ge(f_ln, 2)
            dve.tensor_tensor_scan(fc[FR, :], fone[FR, :], fl[FR, :], 0.0, ALU.mult, ALU.add).then_inc(f_cum, 1)

            def fox_head(h, proj=True, attn=True, fill=None):
                g = h - 1
                for u in range(4 * UPT):
                    if proj:
                        split(U_FOX + u + LO_AHEAD, h, 4 * UPT)
                    elif fill is not None:
                        fill(u)
                    if attn and u == 0:
                        take_tile(T_FOX + 3, U_FOX + 4 * UPT * g + 4 * UPT, z_t, halve=True)
                    if attn and u in (0, 1):
                        r, t, gc = ((sqq, q_t, G_Q), (sqk, k_t, G_K))[u]
                        dve.wait_ge(rms_ready, 2 * g + u + 1)
                        link(dve.reciprocal(r, r))
                        dve.scalar_tensor_tensor(t, t, gcol[:, gc:gc + 1], r, ALU.mult, ALU.mult).then_inc(qk_ready, 1)
                    if attn and u == 2:
                        dve.wait_ge(tz_ready, g + 1)
                        dve.scalar_tensor_tensor(tz_t, tz_t, 1.0, z_t, ALU.add, ALU.mult).then_inc(zs_ready, 1)
                    if attn and u == 3:
                        dve.wait_ge(scores_done, g + 1)
                    if proj and u == 3:
                        take_tile(T_FOX, U_FOX + 4 * UPT * h + 1 * UPT, q_t)
                    if attn and u == 3:
                        dve.wait_ge(ckm_ready, g + 1)
                        for t in range(TB):
                            at, n = prob_at[t], t * P
                            src = score_of(t)
                            c_query = cq[:, t, bass.ds(32 - H + g, 1)]
                            if t:
                                dve.scalar_tensor_tensor(prob[:, at:at + n], src[:, 0:n], c_query, ckb[:, 0:n],
                                                         ALU.add, ALU.subtract)
                            ins = dve.scalar_tensor_tensor(prob[:, at + n:at + n + P], src[:, n:n + P], c_query,
                                                           ckm[:, n:n + P], ALU.add, ALU.subtract)
                        link(ins)
                        for t in range(TB):
                            dve.tensor_reduce(negm[:, t:t + 1], prob[:, prob_at[t]:prob_at[t] + (t + 1) * P],
                                              AX.X, ALU.max, negate=True).then_inc(negm_ready, 1)
                    if proj and u == 4:
                        take_tile(T_FOX + 1, U_FOX + 4 * UPT * h + 2 * UPT, k_t)
                    if attn and u == 5:
                        dve.wait_ge(exp_ready, TB * g + TB)
                        link(dve.reciprocal(rsum, rsum))
                        for t in range(TB):
                            pr = prob[:, prob_at[t]:prob_at[t] + (t + 1) * P]
                            ins = dve.tensor_scalar(pr, pr, rsum[:, t:t + 1], None, ALU.mult)
                        ins.then_inc(probs_ready, 1)
                    if proj and u == 6:
                        take_tile(T_FOX + 2, U_FOX + 4 * UPT * h + 3 * UPT, v_t)
                    if attn and u == 7:
                        dve.wait_ge(pv_done, g + 1)
                        dve.wait_ge(zs_ready, g + 1)
                        dve.tensor_tensor(yT[:, g], bank[5][:, :], tz_t, ALU.mult).then_inc(y_ready, 1)

            def score_of(t):
                return {0: bank[6][:, 384:512], 1: bank[7][:, 0:256], 2: bank[6][:, 0:384], 3: bank[5][:, :]}[t]

            def tree_of(lv):
                if lv == 0:
                    return f_t
                at = S - (S >> (lv - 1))
                return tree[:, at:at + (S >> lv)]

            def hg_head(h, proj=True, attn=True, first=False, fill=None):
                g = h - 1

                def level(lv):
                    n = 1 << lv
                    dve.wait_ge(level_done, LEVELS * g + lv + 1)
                    dve.wait_ge(level_ready, (LEVELS + 1) * g + lv + 1)
                    if lv:
                        dve.wait_ge(att_ready, LEVELS * g + lv)
                    nb = P // (2 * n)
                    t = tree_of(lv).rearrange("p (a x b e) -> p a x b e", x=2, b=nb, e=2)
                    q, k, pairs = (tile.rearrange("p (a x b e n) -> p a x b e n", x=2, b=nb, e=2, n=n)
                                   for tile in (q_t, k_t, att))
                    for x in range(2):
                        ins = dve.tensor_tensor(k[:, :, x, :, x], k[:, :, x, :, x],
                                                t[:, :, x, :, 1 - x:2 - x].to_broadcast([P, TB // 2, nb, n]), ALU.mult)
                    ins.then_inc(keys_ready, 1)
                    for x in range(2):
                        dve.tensor_tensor(q[:, :, x, :, 1 - x], q[:, :, x, :, 1 - x],
                                          t[:, :, x, :, x:x + 1].to_broadcast([P, TB // 2, nb, n]), ALU.mult)
                    both = tree_of(lv).rearrange("p (b e) -> p b e", e=2)
                    dve.tensor_tensor(tree_of(lv + 1), both[:, :, 0], both[:, :, 1], ALU.mult).then_inc(level_ready, 1)
                    for x in range(2):
                        mask = levels[:, lv].rearrange("p (x a b n) -> p x a b n", x=2, a=TB // 2, n=n)[:, x]
                        src = bank[2 + lv % 2][:, 0:S // 2].rearrange("p (a x b n) -> p a x b n", x=2, b=nb, n=n)
                        ins = dve.copy_predicated(pairs[:, :, x, :, 1 - x], mask, src[:, :, x])
                    ins.then_inc(att_ready, 1)

                for u in range(4 * UPT):
                    if attn and u == 0:
                        dve.wait_ge(diag_done, g + 1)
                        dve.tensor_tensor(att.rearrange("p (t n) -> p t n", t=TB),
                                          bank[5][:, :].rearrange("p (t n) -> p t n", t=TB),
                                          ident[:, :].unsqueeze(1).to_broadcast([P, TB, P]), ALU.mult)
                        dve.tensor_tensor(q_t, q_t, f_t, ALU.mult).then_inc(level_ready, 1)
                    if attn and 1 <= u < 4:
                        level(2 * u - 1)
                    if proj:
                        split(U_HG + u + LO_AHEAD, h, 4 * UPT)
                    elif fill is not None:
                        fill(u)
                    if attn and u < 4:
                        level(2 * u)
                    if attn and u == 0:
                        take_tile(T_HG + 3, U_HG + 4 * UPT * g + 4 * UPT, z_t, halve=True)
                    if first and u == 2:
                        token_rinv(2)
                    if proj and u == 2:
                        if attn:
                            dve.wait_ge(hg_vt, g + 1)
                        take_hg_tile(T_HG, U_HG + 4 * UPT * h + 1 * UPT, v_t)
                    if proj and u == 4:
                        take_hg_tile(T_HG + 1, U_HG + 4 * UPT * h + 2 * UPT, f_t)
                    if attn and u == 4:
                        dve.wait_ge(u_done, g + 1)
                        dve.wait_ge(level_ready, (LEVELS + 1) * (g + 1))
                        total = tree_of(LEVELS)
                        link(dve.tensor_copy(st[:, 0:P], bank[5][:, 0:P]))
                        link(dve.scalar_tensor_tensor(st[:, P:2 * P], st[:, 0:P], total[:, 1:2],
                                                      bank[5][:, P:2 * P], ALU.mult, ALU.add))
                        dve.scalar_tensor_tensor(st[:, 2 * P:3 * P], st[:, P:2 * P], total[:, 2:3],
                                                 bank[5][:, 2 * P:3 * P], ALU.mult, ALU.add).then_inc(state_ready, 1)
                    if attn and u == 5:
                        dve.wait_ge(ot_done, g + 1)
                        dve.tensor_copy(chunks(o_t, 0), chunks(bank[6][:, :], 0))
                        dve.tensor_copy(reversed_chunks(o_t), chunks(bank[6][:, :], 1)).then_inc(o_ready, 1)
                    if proj and u == 5:
                        dve.wait_ge(thf_ready, h + 1)
                        link(dve.tensor_scalar(f_t, f_t, 0.5, 0.5, ALU.mult, ALU.add))
                        link(dve.tensor_scalar(f_t, f_t, upper[:, bass.ds(h, 1)], lower[:, bass.ds(h, 1)],
                                               ALU.mult, ALU.add))
                        dve.tensor_scalar(k_t, f_t, -1.0, 1.0, ALU.mult, ALU.add).then_inc(keys_ready, 1)
                    if proj and u == 6:
                        take_hg_tile(T_HG + 2, U_HG + 4 * UPT * h + 3 * UPT, q_t, halve=True)
                    if attn and u == 6:
                        dve.wait_ge(orms_ready, g + 1)
                        link(dve.reciprocal(osq, osq))
                        dve.wait_ge(o_ready, g + 1)
                        dve.scalar_tensor_tensor(o_t, o_t, gcol[:, G_O:G_O + 1], osq, ALU.mult, ALU.mult)
                    if proj and u == 7:
                        dve.wait_ge(tq_ready, h + 1)
                        dve.wait_ge(tile_out, N_HG + 4 * h + 3)
                        dve.scalar_tensor_tensor(q_t, tq_t, 1.0, q_t, ALU.add, ALU.mult).then_inc(hg_qk, 1)
                    if attn and u == 7:
                        dve.wait_ge(hg_tz, g + 1)
                        link(dve.scalar_tensor_tensor(tz_t, tz_t, 1.0, z_t, ALU.add, ALU.mult))
                        dve.tensor_tensor(yT[:, g], o_t, tz_t, ALU.mult).then_inc(y_ready, 1)

            for lay, (head, links) in enumerate(((fox_head, 4), (hg_head, 6))):
                if lay:
                    head(0, attn=False, first=True)
                else:
                    head(0, attn=False)
                linked_loop(1, H, links, head)

                def fill(u, lay=lay):
                    for m in (FOX_LO, HG_LO)[lay].get(u, []):
                        split(U_OUT[lay] + m)
                head(H, proj=False, fill=fill)
                dve.wait_ge(x_ready, KT * (3 * lay + 1) + KT - 1)
                split_one(3 * lay + 1, yT, KT - 1)
                zero_acc()

                def out_pair(i, lay=lay):
                    for j in range(2):
                        k = 2 * i + j
                        if not (isinstance(i, int) and i == 0):
                            for m in range(UPT):
                                split(U_OUT[lay] + UPT * j + m + LO_AHEAD, i, 2 * UPT)
                            if isinstance(i, int) and j:
                                split(U_EM[lay] + EM_UNITS - 1)
                        dve.wait_ge(w_used, U_OUT[lay] + end_of(k))
                        dve.tensor_copy(yT[:, k], bank[T_OUT[lay] % 2 ^ j][:, :]).then_inc(yo_ready, 1)
                        add_square(k, 2 * lay + 1, j)
                out_pair(0)
                loop(dve, 1, KT // 2 - 1, out_pair)
                out_pair(KT // 2 - 1)
                token_rinv(2 * lay + 1)

                def scale_y(k, lay=lay):
                    dve.scalar_tensor_tensor(yT[:, k], yT[:, k], gcol[:, bass.ds(G_POST + KT * lay + k, 1)],
                                             rinv[:, :], ALU.mult, ALU.mult).then_inc(yn_ready, 1)

                def scale_and_split(k, lay=lay):
                    scale_y(k)
                    split_one(3 * lay + 2, hT, k - NORM_LAG)
                for k in range(NORM_LAG):
                    scale_y(k)
                loop(dve, NORM_LAG, 9, scale_and_split)
                dve.wait_ge(lo_done, U_PG[lay] + 2)
                split(U_PG[lay] + 2)
                loop(dve, 9, 11, scale_and_split)
                split(U_PG[lay] + 3)
                loop(dve, 11, KT, scale_and_split)
                for k in range(KT - NORM_LAG, KT):
                    split_one(3 * lay + 2, hT, k)
                    if k >= KT - 2:
                        split(U_PG[lay] + 2 * UPT + k - KT + 2)
                if lay == 0:
                    zero_acc()

                def gate_pair(i, lay=lay, last=False):
                    for j in range(2):
                        k = 2 * i + j
                        if not (isinstance(i, int) and i == 0):
                            for m in range(UPT):
                                split(U_PG[lay] + UPT * j + m + LO_AHEAD, i, 2 * UPT)
                        if last and j == 1:
                            split_scaled(3, G_PRE + KT, 0, 1)
                        dve.wait_ge(tg_ready, KT * lay + k + 1)
                        dve.wait_ge(pe_in[j], 16 * (KT // 2) * lay + 16 * i + 16)
                        link(dve.scalar_tensor_tensor(tg2[j], tg2[j], 1.0, pe2[j], ALU.add, ALU.mult))
                        if lay and not isinstance(i, int):
                            dve.wait_ge(outT_done, k - 1)
                        dst = hout2[j] if lay else hT[:, k]
                        dve.scalar_tensor_tensor(dst, tg2[j], 0.5, hT[:, k], ALU.mult, ALU.add).then_inc(h_new, 1)
                        if last and j == 1:
                            split_scaled(3, G_PRE + KT, 1, 3)
                        if lay == 0:
                            add_square(k, 2, j)
                gate_pair(0)
                if lay == 0:
                    linked_loop(1, KT // 2 - 1, 2, gate_pair)
                    gate_pair(KT // 2 - 1, last=True)
                    split_scaled(3, G_PRE + KT, 3, KT)
                else:
                    linked_loop(1, KT // 2 - 1, 2, gate_pair)
                    dve.wait_ge(outT_done, KT - 2)
                    gate_pair(KT // 2 - 1)

        @block.tensor
        def _(pe):
            def product(dst, u, b, k, first, last):
                hi, lo = whi[:, u % RING, b], wlo[:, u % RING, b]
                pe.matmul(dst, hi, xhi[:, k], start=first, stop=False)
                pe.matmul(dst, hi, xlo[:, k], start=False, stop=False)
                return pe.matmul(dst, lo, xhi[:, k], start=False, stop=last)

            def unit(u, i, per, t0, t, half, freed=tile_out, stage=None, mid=None):
                pe.wait_ge(lo_done, u + per * i + 1)
                if half == 0:
                    if freed is not None:
                        wait(pe, freed, t - 1)
                for b in range(UB):
                    k = UB * half + b
                    if stage is not None:
                        pe.wait_ge(x_ready, KT * stage + k + 1)
                    ins = product(bank[t0 % 2][:, :], u, b, k, k == 0, k == KT - 1)
                    if b == UB // 2 - 1 and mid is not None:
                        mid()
                ins.then_inc(w_used, 1)

            def piece(u0, banks, stage, m, first, last):
                half, j = m // 2, m % 2
                if first == 0:
                    pe.wait_ge(lo_done, u0 + m + 1)
                for b in range(first, last):
                    k = UB * half + b
                    pe.wait_ge(x_ready, KT * stage + k + 1)
                    ins = product(bank[banks[j]][:, :], u0 + m, b, k, k == 0, k == KT - 1)
                    if b == UB - 1:
                        ins.then_inc(w_used, 1)

            def turn(dst, src, n, ins=None):
                for t in range(n):
                    ins = pe.transpose(dst[:, t * P:(t + 1) * P], src[:, t * P:(t + 1) * P], ident[:, :])
                return ins

            def sum_squares(stage, between=None):
                pe.wait_ge(acc_step, (KT - 1) * (stage + 1))
                pe.matmul(bank[7][:, :], ones[:, :], acc, start=True, stop=False)
                if between is not None:
                    between()
                pe.wait_ge(sq_done, KT * (stage + 1))
                pe.matmul(bank[7][:, :], ones[:, :], sq2[1], start=False, stop=True).then_inc(norm_done, 1)

            pe.wait_ge(ident_in, 16)
            for i in range(2):
                pe.wait_ge(p_in[i], 16)
                for k in range(PK):
                    for t in range(TB):
                        at = t * PLE + k * P
                        ins = pe.transpose(bank[2 + PK * i + k][:, t * P:(t + 1) * P],
                                           pstage[i][:, at:at + P], ident[:, :])
                    ins.then_inc(pt_p, 1)
            pe.wait_ge(gvec_in, 96)
            pe.transpose(bank[7][:, 0:G_ROWS], grow[0:G_ROWS, :], ident[0:G_ROWS, 0:G_ROWS]).then_inc(g_turned, 1)
            pe.wait_ge(p_ready, PK)

            def turn_x(k):
                pe.wait_ge(x_in[k % 4], 16 * (k // 4) + 16)
                wait(pe, sq_done, k - 1)
                turn(bank[2 + k % 2], xstage[k % 4], TB).then_inc(x_turned, 1)
            for u in range(PE_UNITS):
                pe.wait_ge(lo_done, u + 1)
                for f in range(4):
                    if u == 0 and f == 2:
                        pe.wait_ge(p_staged, PK)
                    wait(pe, tile_out, 4 * u + f - 3)
                    for k in range(PK):
                        ins = product(bank[embed_banks[f]][:, :], u, 4 * k + f, KT - PK + k, k == 0, k == PK - 1)
                    ins.then_inc(embed_done if f < 3 else w_used, 1)
                    turn_x(4 * u + f)
            unit(U_F, 0, 0, T_F, T_F, 0, stage=0)
            sum_squares(0)
            unit(U_F + 1, 0, 0, T_F, T_F, 1, stage=0)
            def turn_c():
                pe.wait_ge(f_cum, 1)
                for t in range(TB):
                    ins = pe.transpose(bank[6][:, 32 * t:32 * (t + 1)], fc[FR, t * P:(t + 1) * P], ident[FR, FR])
                ins.then_inc(f_turned, 1)

            def fox_head(h, proj=True, attn=True, first=False, fill=None):
                g = h - 1
                for u in range(4 * UPT):
                    if attn and u == 0:
                        pe.wait_ge(tile_out, T_FOX + 4 * g + 3)
                        turn(bank[4], v_t, TB).then_inc(vt_done, 1)
                        for n, sq in enumerate((sqq, sqk)):
                            pe.wait_ge(sq_ready, 2 * g + n + 1)
                            pe.matmul(bank[2 + n][:, :], ones[:, :], sq, start=True, stop=True).then_inc(stats_done, 1)
                    if proj:
                        j = u // UPT
                        unit(U_FOX + u, h, 4 * UPT, T_FOX + j, T_FOX + 4 * h + j, u % UPT)
                    elif fill is not None:
                        fill(u)
                    if first and u == 3:
                        turn_c()
                    if attn and u == 2:
                        pe.wait_ge(qk_ready, 2 * g + 2)
                        pe.wait_ge(tile_out, T_FOX + 4 * g + 4)
                        for t in range(TB):
                            n = (t + 1) * P
                            dst = {0: bank[6][:, 384:512], 1: bank[7][:, 0:256],
                                   2: bank[6][:, 0:384], 3: bank[5][:, :]}[t]
                            ins = pe.matmul(dst, q_t[:, t * P:n], k_t[:, 0:n], start=True, stop=True)
                        ins.then_inc(scores_done, 1)
                    if attn and u == 5:
                        pe.wait_ge(probs_ready, g + 1)
                        pe.wait_ge(vtok_ready, g + 1)
                        dsts = [bank[2][:, :], bank[3][:, 0:384], bank[4][:, 0:256], bank[3][:, 384:512]]
                        for kb in range(TB):
                            for t in range(kb, TB):
                                at = prob_at[t] + kb * P
                                ins = pe.transpose(dsts[kb][:, (t - kb) * P:(t - kb + 1) * P],
                                                   prob[:, at:at + P], ident[:, :])
                        ins.then_inc(pt_done, 1)
                    if attn and u == 6:
                        pe.wait_ge(pt_ready, g + 1)
                        for kb in range(TB):
                            n = S - kb * P
                            ins = pe.matmul(bank[5][:, kb * P:S], vtok[:, kb * P:(kb + 1) * P],
                                            probT[:, probT_at[kb]:probT_at[kb] + n],
                                            start=(kb == 0), stop=(kb == TB - 1))
                        ins.then_inc(pv_done, 1)

            def hg_head(h, proj=True, attn=True, first=False, fill=None):
                g = h - 1

                def level(lv):
                    n = 1 << lv
                    nb = P // (2 * n)
                    pe.wait_ge(kmix_ready, LEVELS * g + lv + 1)
                    pe.wait_ge(level_ready, (LEVELS + 1) * g + lv + 1)
                    if lv >= 2:
                        pe.wait_ge(att_ready, LEVELS * g + lv - 1)
                    for pair in range(TB // 2):
                        at = 2 * P * pair
                        queries = bass.AP(q_t.tensor, q_t.offset + at + n,
                                          [list(q_t.ap[0]), [P - n, 2], [2 * n, nb], [1, n]])
                        ins = pe.matmul(bank[2 + lv % 2][:, pair * P:(pair + 1) * P], kmix[:, pair], queries,
                                        start=True, stop=True)
                    ins.then_inc(level_done, 1)

                def slot(n):
                    if n == 0:
                        pe.wait_ge(tile_out, N_HG + 4 * g + 1)
                        turn(bank[4], v_t, TB).then_inc(hg_vt, 1)
                        pe.wait_ge(hg_qk, g + 1)
                        for t in range(TB):
                            c = slice(t * P, (t + 1) * P)
                            ins = pe.matmul(bank[5][:, c], k_t[:, c], q_t[:, c], start=True, stop=True)
                        ins.then_inc(diag_done, 1)
                    if 1 <= n <= LEVELS:
                        level(n - 1)
                    if n == 8:
                        pe.wait_ge(level_ready, (LEVELS + 1) * (g + 1))
                        pe.wait_ge(hg_vtok, g + 1)
                        turn(bank[4], k_t, TB - 1).then_inc(kst_done, 1)
                    if n == 9:
                        pe.wait_ge(kst_ready, g + 1)
                        for t in range(TB - 1):
                            c = slice(t * P, (t + 1) * P)
                            ins = pe.matmul(bank[5][:, c], kst[:, c], vtok[:, c], start=True, stop=True)
                        ins.then_inc(u_done, 1)
                    if n == 10:
                        pe.wait_ge(state_ready, g + 1)
                        pe.wait_ge(att_ready, LEVELS * (g + 1))
                        for t in range(TB):
                            c = slice(t * P, (t + 1) * P)
                            ins = pe.matmul(bank[6][:, c], vtok[:, c], att[:, c], start=True, stop=(t == 0))
                            if t:
                                ins = pe.matmul(bank[6][:, c], st[:, (t - 1) * P:t * P], q_t[:, c],
                                                start=False, stop=True)
                        ins.then_inc(ot_done, 1)
                    if n == 12:
                        pe.wait_ge(osq_ready, g + 1)
                        pe.matmul(bank[7][:, :], ones[:, :], osq, start=True, stop=True).then_inc(ostat_done, 1)

                for u in range(4 * UPT):
                    if attn:
                        slot(2 * u)
                    if proj:
                        j = u // UPT
                        unit(U_HG + u, h, 4 * UPT, T_HG + j, N_HG + 4 * h + j, u % UPT,
                             stage=3 if first and j == 0 else None,
                             mid=(lambda u=u: slot(2 * u + 1)) if attn else None)
                    elif attn:
                        fill(2 * u)
                        slot(2 * u + 1)
                        fill(2 * u + 1)
                    if first and u == 1:
                        sum_squares(2)

            for lay, head in enumerate((fox_head, hg_head)):
                head(0, attn=False, first=True)
                loop(pe, 1, H, head)

                def fill(n, lay=lay):
                    for m, b0, b1 in (FOX_FILL, HG_FILL)[lay].get(n, []):
                        if (m, b0) == (1, 0):
                            pe.wait_ge(tile_out, (T_FOX, N_HG)[lay] + 4 * H)
                        piece(U_OUT[lay], [T_OUT[lay] % 2, T_OUT[lay] % 2 ^ 1], 3 * lay + 1, m, b0, b1)
                head(H, proj=False, fill=fill)
                for m in (2, 3):
                    piece(U_OUT[lay], [T_OUT[lay] % 2, T_OUT[lay] % 2 ^ 1], 3 * lay + 1, m, UB - 1, UB)

                def out_pair(i, lay=lay):
                    for j in range(2):
                        for half in range(UPT):
                            unit(U_OUT[lay] + UPT * j + half, i, 2 * UPT, T_OUT[lay] + j,
                                 2 * i + j + KT * lay, half, freed=yo_ready)
                loop(pe, 1, KT // 2, out_pair)

                def embed_tile(a, f, lay=lay):
                    n = KT // 2 * lay + 4 * a + f
                    up = (U_EM[lay] + EM_UNITS - 1) % RING
                    phi, plo = (w[:, up].rearrange("p (k c) n -> p k (c n)", k=PK) for w in (whi, wlo))
                    if f == 0:
                        pe.wait_ge(lo_done, U_PG[lay])
                    if a:
                        pe.wait_ge(em_out, n - 3)
                    for k in range(PK):
                        ring = (U_EM[lay] + a) % RING
                        hi, lo = whi[:, ring, 4 * k + f], wlo[:, ring, 4 * k + f]
                        dst = bank[later_banks[f]][:, :]
                        pe.matmul(dst, hi, phi[:, k], start=k == 0, stop=False)
                        pe.matmul(dst, hi, plo[:, k], start=False, stop=False)
                        ins = pe.matmul(dst, lo, phi[:, k], start=False, stop=k == PK - 1)
                    if f < 3:
                        ins.then_inc(embed_done, 1)
                    else:
                        ins.then_inc(w_used, 1 + a)
                sum_squares(2 * lay + 1, between=lambda: embed_tile(0, 0))
                for n in range(1, KT // 2):
                    embed_tile(n // 4, n % 4)

                for m in (0, 2):
                    for b in range(UB):
                        for j in range(2):
                            piece(U_PG[lay], GATE_BANKS, 3 * lay + 2, m + j, b, b + 1)

                def gate_pair(i, lay=lay):
                    for j in range(2):
                        k = 2 * i + j
                        for half in range(UPT):
                            unit(U_PG[lay] + UPT * j + half, i, 2 * UPT, T_PG[lay] + j,
                                 k + KT * lay, half, freed=None if isinstance(i, int) else tg_ready)
                            if lay:
                                if isinstance(i, int) and j == 0:
                                    turn_out(half, half)
                                elif half == 0:
                                    turn_out(k - 1, 1 - j)

                def turn_out(k, slot):
                    pe.wait_ge(h_new, KT + k + 1)
                    wait(pe, out_staged, k - 1)
                    turn(bank[2 + slot], hout2[slot], TB).then_inc(outT_done, 1)
                gate_pair(1)
                loop(pe, 2, KT // 2, gate_pair)
                if lay:
                    turn_out(KT - 1, 1)


_INS = ["x", "p", "w_in_fox", "b_f_fox", "g_q_fox", "g_k_fox", "w_out_fox", "w_in_hg", "lb_logits", "g_o_hg",
        "w_out_hg", "pre_norm", "post_norm", "w_pe", "w_pg"]


def kernel(**inputs):
    import numpy as _np
    import concourse.bacc as _bacc
    from concourse import mybir as _mybir
    from concourse.bass_utils import run_bass_kernel_spmd as _run

    ident = _np.eye(P, dtype=_np.float32)
    causal = _np.where(_np.arange(P)[None, :] <= _np.arange(P)[:, None], 0.0, NEG).astype(_np.float32)
    levels = _np.zeros((P, LEVELS, 2, P // 2), _np.float32)
    for lv in range(LEVELS):
        n = 1 << lv
        s = _np.arange(P)[:, None]
        b = _np.arange(P // 2)[None, :] // n
        for x in range(2):
            levels[:, lv, x] = (s // (2 * n) == b) & (s // n % 2 == x)
    consts = {"c_ident": ident, "c_causal": causal, "c_levels": levels.reshape(P, -1)}

    nc = _bacc.Bacc("TRN2", target_bir_lowering=False, num_devices=1)
    arrays, args = {}, []
    for name in _INS + list(consts):
        a = consts[name] if name in consts else _np.ascontiguousarray(inputs[name])
        arrays[f"in_{name}_dram"] = a
        args.append(nc.dram_tensor(f"in_{name}_dram", a.shape, _mybir.dt.from_np(a.dtype), kind="ExternalInput").ap())
    args.append(nc.dram_tensor("out_0_dram", (1, S, D), _mybir.dt.float32, kind="ExternalOutput").ap())
    trunk(nc, *args)
    r = _run(nc, [arrays], core_ids=[0])
    return r.results[0]["out_0_dram"]
```
